# Optimizing a Trainium2 kernel written in Bass

```python
import math
import jax, jax.numpy as jnp
from jax import lax
import numpy as np

D_MODEL = 2048
BATCH = 1
SEQ = 256
DEPTH = 1

D_MIX = D_MODEL
D_DIFF = D_MIX // 2
D_HGRN = D_MIX - D_DIFF
DIFF_HEAD_DIM = 128
DIFF_QK_DIM = DIFF_HEAD_DIM // 2
N_DIFF_HEADS = D_DIFF // DIFF_HEAD_DIM
HGRN_HEAD_DIM = 128
N_HGRN_HEADS = D_HGRN // HGRN_HEAD_DIM
HGRN_CHUNK = 64
Q_BLOCK = 128
NUM_BUCKETS = 32
MAX_DISTANCE = 128
N_EXPERTS = 16
N_GROUPS = 4
EXPERTS_PER_GROUP = N_EXPERTS // N_GROUPS
TOP_K = 2
D_EXPERT = D_MODEL // 4
N_MOD = 6
EPS = 1e-6
IN_COLS = 3 * D_DIFF + 4 * D_HGRN
SPLITS = [D_DIFF, 2 * D_DIFF, 3 * D_DIFF, 3 * D_DIFF + D_HGRN, 3 * D_DIFF + 2 * D_HGRN, 3 * D_DIFF + 3 * D_HGRN]

kernel_name = "hybrid_diffattn_hgrn2_groupedmoe_adaln"

def rms_norm(x, g):
    xf = x.astype(jnp.float32)
    y = xf * lax.rsqrt(jnp.mean(xf * xf, axis=-1, keepdims=True) + EPS)
    return (y * g.astype(jnp.float32)).astype(x.dtype)

def t5_bucket(n):
    max_exact = NUM_BUCKETS // 2
    nf = jnp.maximum(n, 1).astype(jnp.float32)
    large = max_exact + (jnp.log(nf / max_exact) / math.log(MAX_DISTANCE / max_exact)
                         * (NUM_BUCKETS - max_exact)).astype(jnp.int32)
    large = jnp.minimum(large, NUM_BUCKETS - 1)
    return jnp.where(n < max_exact, n, large)

def diff_attention(q, k, v, rel_table, lam, lambda_init, subln_g):
    B, S = q.shape[0], q.shape[1]
    nb = S // Q_BLOCK
    H2 = 2 * N_DIFF_HEADS
    qf = q.astype(jnp.float32) * (DIFF_QK_DIM ** -0.5)
    kf = k.astype(jnp.float32)
    vf = v.astype(jnp.float32)
    lam = lam.astype(jnp.float32)
    q_blocks = qf.reshape(B, nb, Q_BLOCK, H2, DIFF_QK_DIM).transpose(1, 0, 2, 3, 4)
    kpos = jnp.arange(S)

    def one_block(args):
        qb, blk = args
        qpos = blk * Q_BLOCK + jnp.arange(Q_BLOCK)
        rel = qpos[:, None] - kpos[None, :]
        causal = rel >= 0
        bias = rel_table.astype(jnp.float32)[t5_bucket(jnp.maximum(rel, 0))]
        s = jnp.einsum('bqhd,bkhd->bhqk', qb, kf) + bias.transpose(2, 0, 1)[None]
        s = jnp.where(causal[None, None], s, -1e30)
        p = jax.nn.softmax(s, axis=-1).reshape(B, N_DIFF_HEADS, 2, Q_BLOCK, S)
        a = p[:, :, 0] - lam * p[:, :, 1]
        return jnp.einsum('bhqk,bkhd->bqhd', a, vf)

    o = lax.map(one_block, (q_blocks, jnp.arange(nb)))
    o = o.transpose(1, 0, 2, 3, 4).reshape(B, S, N_DIFF_HEADS, DIFF_HEAD_DIM)
    o = rms_norm(o, subln_g) * (1.0 - lambda_init)
    return o.reshape(B, S, D_DIFF)

def hgrn2(q, f_raw, v, g, lb, norm_g):
    B, S, _ = q.shape
    H, dk, C = N_HGRN_HEADS, HGRN_HEAD_DIM, HGRN_CHUNK
    nc = S // C
    lbf = lb.astype(jnp.float32)
    fr = f_raw.astype(jnp.float32)
    f = lbf + (1.0 - lbf) * jax.nn.sigmoid(fr)
    log_f = jnp.log(jnp.maximum(f, jnp.finfo(jnp.float32).tiny))
    k = (1.0 - lbf) * jax.nn.sigmoid(-fr)

    def chunks(t):
        return t.astype(jnp.float32).reshape(B, nc, C, H, dk).transpose(1, 0, 3, 2, 4)

    xs = (chunks(q), chunks(k), chunks(v), chunks(log_f))
    causal = jnp.tril(jnp.ones((C, C), dtype=bool))[:, :, None]

    def step(state, inp):
        qc, kc, vc, lc = inp
        b = jnp.cumsum(lc, axis=2)
        b_end = b[:, :, -1:, :]
        o_inter = jnp.einsum('bhtd,bhdv->bhtv', qc * jnp.exp(b), state)
        rel = b[:, :, :, None, :] - b[:, :, None, :, :]
        decay = jnp.where(causal, jnp.exp(jnp.minimum(rel, 0.0)), 0.0)
        scores = jnp.einsum('bhtd,bhsd,bhtsd->bhts', qc, kc, decay)
        o_intra = jnp.einsum('bhts,bhsv->bhtv', scores, vc)
        new_state = (jnp.exp(b_end[:, :, 0, :])[..., None] * state
                     + jnp.einsum('bhsd,bhsv->bhdv', kc * jnp.exp(b_end - b), vc))
        return new_state, o_inter + o_intra

    state0 = jnp.zeros((B, H, dk, dk), jnp.float32)
    _, o = lax.scan(step, state0, xs)
    o = o.transpose(1, 0, 3, 2, 4).reshape(B, S, H, dk)
    o = rms_norm(o, norm_g).reshape(B, S, D_HGRN)
    return o * jax.nn.silu(g.astype(jnp.float32))

def grouped_moe(h, w_router, b_router, w_gate, w_up, w_down):
    B, S, D = h.shape
    t = h.reshape(B * S, D)
    logits = (t @ w_router).astype(jnp.float32) + b_router.astype(jnp.float32)
    probs = jax.nn.softmax(logits, axis=-1)
    grouped = probs.reshape(-1, N_GROUPS, EXPERTS_PER_GROUP)
    group_score = lax.top_k(grouped, TOP_K)[0].sum(-1)
    group_sel = jnp.argmax(group_score, axis=-1)
    expert_mask = jnp.repeat(jax.nn.one_hot(group_sel, N_GROUPS, dtype=jnp.bool_), EXPERTS_PER_GROUP, axis=-1)
    masked = jnp.where(expert_mask, probs, -1.0)
    top_vals, top_idx = lax.top_k(masked, TOP_K)
    weights = top_vals / jnp.sum(top_vals, axis=-1, keepdims=True)
    gates = jnp.sum(jax.nn.one_hot(top_idx, N_EXPERTS, dtype=jnp.float32) * weights[..., None], axis=-2)
    hg = jnp.einsum('td,edf->tef', t, w_gate)
    hu = jnp.einsum('td,edf->tef', t, w_up)
    act = jax.nn.silu(hg) * hu * gates[..., None].astype(hg.dtype)
    y = jnp.einsum('tef,efd->td', act, w_down)
    return y.reshape(B, S, D)

def setup_inputs(seed: int = 0) -> dict:
    key = jax.random.key(seed)
    ks = jax.random.split(key, 24)
    f32 = jnp.float32
    nrm = lambda k, shape, s: jax.random.normal(k, shape, f32) * s
    return {
        "x": nrm(ks[0], (BATCH, SEQ, D_MODEL), 1.0),
        "c": nrm(ks[1], (BATCH, D_MODEL), 1.0),
        "w_in": nrm(ks[2], (DEPTH, D_MODEL, IN_COLS), D_MODEL ** -0.5),
        "w_out": nrm(ks[3], (DEPTH, D_MIX, D_MODEL), D_MIX ** -0.5),
        "attn_norm": 1.0 + nrm(ks[4], (DEPTH, D_MODEL), 0.02),
        "ffn_norm": 1.0 + nrm(ks[5], (DEPTH, D_MODEL), 0.02),
        "w_ada": nrm(ks[6], (DEPTH, D_MODEL, N_MOD * D_MODEL), 0.2 * D_MODEL ** -0.5),
        "b_ada": nrm(ks[7], (DEPTH, N_MOD * D_MODEL), 0.02),
        "lambda_q1": nrm(ks[8], (DEPTH, DIFF_QK_DIM), 0.1),
        "lambda_k1": nrm(ks[9], (DEPTH, DIFF_QK_DIM), 0.1),
        "lambda_q2": nrm(ks[10], (DEPTH, DIFF_QK_DIM), 0.1),
        "lambda_k2": nrm(ks[11], (DEPTH, DIFF_QK_DIM), 0.1),
        "diff_subln": 1.0 + nrm(ks[12], (DEPTH, DIFF_HEAD_DIM), 0.02),
        "hgrn_lb": 1.0 + nrm(ks[13], (DEPTH, D_HGRN), 0.1),
        "hgrn_norm": 1.0 + nrm(ks[14], (DEPTH, HGRN_HEAD_DIM), 0.02),
        "rel_bias": nrm(ks[15], (NUM_BUCKETS, 2 * N_DIFF_HEADS), 0.5),
        "w_router": nrm(ks[16], (D_MODEL, N_EXPERTS), D_MODEL ** -0.5),
        "b_router": nrm(ks[17], (N_EXPERTS,), 0.01),
        "w_gate": nrm(ks[18], (DEPTH, N_EXPERTS, D_MODEL, D_EXPERT), D_MODEL ** -0.5),
        "w_up": nrm(ks[19], (DEPTH, N_EXPERTS, D_MODEL, D_EXPERT), D_MODEL ** -0.5),
        "w_down": nrm(ks[20], (DEPTH, N_EXPERTS, D_EXPERT, D_MODEL), D_EXPERT ** -0.5),
        "final_norm": 1.0 + nrm(ks[21], (D_MODEL,), 0.02),
    }

def reference(x, c, w_in, w_out, attn_norm, ffn_norm, w_ada, b_ada, lambda_q1, lambda_k1, lambda_q2, lambda_k2,
              diff_subln, hgrn_lb, hgrn_norm, rel_bias, w_router, b_router, w_gate, w_up, w_down, final_norm):
    B, S, _ = x.shape
    lb_soft = jax.nn.softmax(hgrn_lb.astype(jnp.float32), axis=0)
    lower_bounds = jnp.maximum(jnp.cumsum(lb_soft, axis=0) - lb_soft[0:1], 0.0)
    c_act = jax.nn.silu(c)
    for l in range(DEPTH):
        mod = c_act @ w_ada[l] + b_ada[l]
        shift1, scale1, gate1, shift2, scale2, gate2 = jnp.split(mod, N_MOD, axis=-1)
        h = rms_norm(x, attn_norm[l]) * (1.0 + scale1[:, None]) + shift1[:, None]
        proj = h @ w_in[l]
        qd, kd, vd, qh, fh, ih, gh = jnp.split(proj, SPLITS, axis=-1)
        lambda_init = 0.8 - 0.6 * math.exp(-0.3 * l)
        lam = (jnp.exp(jnp.sum(lambda_q1[l].astype(jnp.float32) * lambda_k1[l].astype(jnp.float32)))
               - jnp.exp(jnp.sum(lambda_q2[l].astype(jnp.float32) * lambda_k2[l].astype(jnp.float32)))
               + lambda_init)
        attn_out = diff_attention(qd.reshape(B, S, 2 * N_DIFF_HEADS, DIFF_QK_DIM),
                                  kd.reshape(B, S, 2 * N_DIFF_HEADS, DIFF_QK_DIM),
                                  vd.reshape(B, S, N_DIFF_HEADS, DIFF_HEAD_DIM),
                                  rel_bias, lam, lambda_init, diff_subln[l])
        hgrn_out = hgrn2(qh, fh, ih, gh, lower_bounds[l], hgrn_norm[l])
        mixed = jnp.concatenate([attn_out.astype(h.dtype), hgrn_out.astype(h.dtype)], axis=-1) @ w_out[l]
        x = x + gate1[:, None] * mixed
        h2 = rms_norm(x, ffn_norm[l]) * (1.0 + scale2[:, None]) + shift2[:, None]
        x = x + gate2[:, None] * grouped_moe(h2, w_router, b_router, w_gate[l], w_up[l], w_down[l])
    return rms_norm(x, final_norm)


_drawn_inputs = setup_inputs


def setup_inputs(seed=0):
    import zlib

    import numpy as np

    out = dict(_drawn_inputs(seed))
    spreads = {}
    factors = {'attn_norm': 8.0,
     'ffn_norm': 4.635,
     'lambda_q1': 5.792,
     'lambda_k1': 8.0,
     'lambda_q2': 8.0,
     'lambda_k2': 3.996,
     'diff_subln': 8.0,
     'hgrn_norm': 8.0,
     'b_router': 8.0,
     'final_norm': 2.761}
    for name, (base, spread) in spreads.items():
        noise = np.random.default_rng([zlib.crc32(name.encode()), seed]).standard_normal(out[name].shape)
        drawn = base * np.exp(spread * noise) if base else spread * noise
        out[name] = __import__('jax').numpy.asarray(drawn.astype(out[name].dtype))
    for name, factor in factors.items():
        out[name] = (out[name] * factor).astype(out[name].dtype)
    return out
```

```python
import math
from contextlib import ExitStack

import numpy as np

import concourse.bass as bass
from concourse import mybir

F32 = mybir.dt.float32
I32 = mybir.dt.int32
U8 = mybir.dt.uint8
ALU = mybir.AluOpType
ACT = mybir.ActivationFunctionType
AX = mybir.AxisListType.X

P = 128
D = 2048
SEQ = 256
NT = SEQ // P
KT = D // P
PANEL = 512
NP_D = D // PANEL
HD = 128
D_DIFF = D // 2
D_HGRN = D - D_DIFF
NH = D_DIFF // HD
GH = PANEL // HD
NG = NH // GH
QK = HD // 2
CHUNK = 64
BUCKETS = 32
MAX_DISTANCE = 128
NE = 16
NGRP = 4
EPG = NE // NGRP
DE = D // 4
FT = DE // P
CAP = P // 2
NPAIR = NE // 2
ROUNDS = SEQ // CAP
EPS = 1e-6
LAMBDA_INIT = 0.8 - 0.6 * math.exp(-0.3 * 0)
CLAMP = 87.0
SPLIT = 2.0 ** -63
TINY = float(np.finfo(np.float32).tiny)
BIAS_W = 3 * P

COL_QD, COL_KD, COL_VD = 0, D_DIFF, 2 * D_DIFF
COL_QH = 3 * D_DIFF
COL_FH, COL_IH, COL_GH = COL_QH + D_HGRN, COL_QH + 2 * D_HGRN, COL_QH + 3 * D_HGRN

LEVELS = [0, 32, 16, 8, 4, 2, 1, 64]

PER_HGRN, PER_DIFF, PER_EXPERTS = 27 + 4 * 14, 24 + 3 * 14, 11

ROW_C, ROW_AN, ROW_FN, ROW_LB, ROW_SUB, ROW_HN, N_ROWS = 0, 16, 32, 48, 56, 57, 58


def shape_constants():
    n = np.arange(P)
    ident = np.eye(P, dtype=np.float32)
    before = (n[:, None] < n[None, :]).astype(np.float32)
    slot = np.broadcast_to(np.tile(np.arange(CAP), 2)[None, :], (P, P)).astype(np.float32)
    rank = np.broadcast_to(np.concatenate([NE - np.arange(NE), NGRP - np.arange(NGRP)])[None, :], (P, NE + NGRP))
    consts = np.concatenate([ident, before, slot, rank.astype(np.float32)], axis=1)
    masks = []
    for half in LEVELS:
        if half == 0:
            m = n[:, None] == n[None, :]
        else:
            m = (n[:, None] // (2 * half) == n[None, :] // (2 * half)) & (n[:, None] // half % 2 == 0) & (n[None, :] // half % 2 == 1)
        masks.append(m.astype(np.float32))
    masks = np.ascontiguousarray(np.stack(masks, axis=1).reshape(P, len(LEVELS) * P))
    rel = 2 * P - 1 - np.arange(BIAS_W)
    exact = BUCKETS // 2
    far = np.maximum(rel, 1).astype(np.float32)
    large = exact + (np.log(far / np.float32(exact)) / np.float32(math.log(MAX_DISTANCE / exact)) * (BUCKETS - exact)).astype(np.int32)
    bucket = np.where(rel < exact, np.maximum(rel, 0), np.minimum(large, BUCKETS - 1))
    onehot = np.zeros((BUCKETS + 1, BIAS_W), np.float32)
    onehot[bucket, np.arange(BIAS_W)] = 1.0
    onehot[:, rel < 0] = 0.0
    onehot[BUCKETS, rel < 0] = -1e30
    return consts, masks, onehot


class Chain:

    def __init__(self, eng, sem):
        self.eng, self.sem, self.n, self.turns = eng, sem, 0, 0

    def step(self, ins):
        ins.then_inc(self.sem, 1)
        self.n += 1

    def wait(self):
        self.eng.wait_ge(self.sem, self.turns + self.n)

    def link(self, ins):
        self.step(ins)
        self.wait()

    def enter(self, i, per):
        self.before, self.per, self.outer = self.n, per, self.turns
        self.turns = self.turns + i * per

    def leave(self, times):
        assert self.n - self.before == self.per, (self.sem, self.n - self.before)
        self.n += self.per * (times - 1)
        self.turns = self.outer


def build_program(nc, x, c, w_in, w_out, attn_norm, ffn_norm, w_ada, b_ada, lambda_q1, lambda_k1, lambda_q2,
                  lambda_k2, diff_subln, hgrn_lb, hgrn_norm, rel_bias, w_router, b_router, w_gate, w_up, w_down,
                  final_norm, consts, masks, onehot, out):
    with ExitStack() as ctx:
        def sb(name, shape, dt=F32):
            return ctx.enter_context(nc.sbuf_tensor(name, shape, dt))

        def sem(name):
            return ctx.enter_context(nc.semaphore(name))

        SLOT = 8 * PANEL
        ring = sb("ring", [P, 6, SLOT])
        res = sb("res", [P, NT, D])
        hT = sb("hT", [P, KT, SEQ])
        mixT = sb("mixT", [P, KT, SEQ])
        gates_bc = sb("gates_bc", [P, 2 * D])
        work = sb("work", [P, 7168])
        cst = sb("cst", [P, 3 * P + NE + NGRP])
        msk = sb("msk", [P, len(LEVELS), P], U8)
        ones = sb("ones", [P, P])
        mean_w = sb("mean_w", [P, P])
        ccol = sb("ccol", [P, KT])
        cact = sb("cact", [P, KT, 32])
        resets = sb("resets", [P, SEQ])
        rows = sb("rows", [N_ROWS, P])
        brows = sb("brows", [64, P])
        cols = sb("cols", [P, N_ROWS])
        bcols = sb("bcols", [P, 64])
        mod = sb("mod", [P, 64])
        a_mul = sb("a_mul", [P, 2 * KT])
        lb = sb("lb", [P, 5, NH])
        lam = sb("lam", [1, 4, QK])
        lams = sb("lams", [1, 8])
        stat = sb("stat", [P, 64])
        count_i = sb("count_i", [1, 2], I32)
        relb = sb("relb", [BUCKETS + 1, 2 * NH])
        nhalf = sb("nhalf", [P, 1])
        waiter = sb("waiter", [1, 2 * len(LEVELS)])

        ident = cst[:, 0:P]
        before = cst[:, P:2 * P]
        slot_id = cst[:, 2 * P:3 * P]
        rank16 = cst[:, 3 * P:3 * P + NE]
        rank4 = cst[:, 3 * P + NE:3 * P + NE + NGRP]

        head = ring[:, 4:6, :].rearrange("p a (b n) -> p (a b) n", n=GH * SEQ)

        def hbuf(n):
            return head[:, n, :]

        qd, kd, vd, qh, kh, bh, gh, vh = (hbuf(n) for n in range(8))
        heads = lambda t: t.rearrange("p (h t) -> p h t", h=GH)
        toks = lambda t: t.rearrange("p (m n) -> p m n", m=NT)
        panelv = lambda s: ring[:, s, :].rearrange("p (k n) -> p k n", n=PANEL)
        dbuf = [work[:, 0:1024], work[:, 1024:2048]]
        zbuf = [work[:, 2048:3072], work[:, 3072:4096]]
        sc_diag = work[:, 4096:5120]
        sc_off = work[:, 5120:5632]
        ohb = work[:, 5632:6656]
        sbuf = work[:, 0:1536].rearrange("p (b s n) -> p b s n", b=2, s=2)
        bias = work[:, 1536:3072].rearrange("p (b s n) -> p b s n", b=2, s=2)
        aT = work[:, 3072:4608].rearrange("p (h n) -> p h n", h=GH)
        odb = work[:, 4608:5632]
        amix = work[:, 5632:6016]
        osq_d = work[:, 0:1024]
        rs_d = work[:, 5632:6656]
        tmp = work[:, 4608:5120]
        arow = [sb("arow", [P, PANEL])[:, :], work[:, 6656:7168]]
        xn = mixT[:, :, :].rearrange("p k t -> p (k t)").rearrange("p (m n) -> p m n", m=NT)
        xn2 = hT[:, :, :].rearrange("p k t -> p (k t)").rearrange("p (m n) -> p m n", m=NT)
        h2T = mixT
        xe = work[:, 0:2048].rearrange("p (k s) -> p k s", k=KT)
        ys = work[:, 2048:4096]
        sel = work[:, 4096:4352].rearrange("p (m s) -> p m s", m=NT)
        selg = work[:, 4352:4608].rearrange("p (m s) -> p m s", m=NT)
        selT = work[:, 4608:4864]
        hid = work[:, 4864:5376]
        hidT = work[:, 5376:5888].rearrange("p (f s) -> p f s", f=FT)
        ytmp = work[:, 5888:6400]
        wr = work[:, 6400:6656].rearrange("p (k e) -> p k e", k=KT)
        lt = work[0:NE, 6656:6912]
        fnorm = gates_bc[:, 0:D]
        rt = ring[:, 5, :]

        def rview(n, w):
            return rt[:, n:n + w]

        logit = rview(0, 32).rearrange("p (m e) -> p m e", m=NT)
        brt = rview(32, 16)
        prob = rview(64, 32).rearrange("p (m e) -> p m e", m=NT)
        pair1 = rview(96, 48).rearrange("p (g q) -> p g q", q=6)
        gsc = rview(144, 8)
        gtmp = rview(152, 8)
        msk4 = rview(160, 8)
        masked = rview(192, 32).rearrange("p (m e) -> p m e", m=NT)
        top1 = rview(224, 32).rearrange("p (m e) -> p m e", m=NT)
        top2 = rview(256, 32).rearrange("p (m e) -> p m e", m=NT)
        t16 = rview(288, 32).rearrange("p (m e) -> p m e", m=NT)
        chosen = rview(320, 32).rearrange("p (m e) -> p m e", m=NT)
        pos = sb("pos", [P, NT, NE + 2])
        gate = sb("gate", [P, NT, NE + 2])

        bias_rows = nc.dram_tensor("bias_rows", (2 * NH, BIAS_W), F32, kind="Internal")

        bank = [ctx.enter_context(nc.psum_tensor(f"bank{b}", [P, PANEL], F32)) for b in range(8)]
        pw = bank[0:4]
        acc, aux = bank[4], bank[5]
        hx = bank[6:8]

        s_x = sem("x_loaded")
        s_small = sem("vectors_loaded")
        s_bload = sem("gate_bias_loaded")
        s_const, mask_ready = sem("constants_set"), sem("masks_ready")
        full = [sem(f"slot{s}_full") for s in range(4)]
        ada_full = [sem(f"slot{s}_full_of_ada") for s in range(2)]
        free = {s: sem(f"slot{s}_free") for s in (0, 2)}
        efull = [sem(f"expert_slot{s}_full") for s in range(6)]
        efree = [sem(f"expert_slot{s}_free") for s in range(6)]
        ada_a, ada_b = sem("ada_panel_a_done"), sem("ada_panel_b_done")
        ada_copied = sem("ada_row_copied")
        aux_full, aux_read = sem("aux_full"), sem("aux_read")
        hx_full = [sem(f"hx{b}_full") for b in range(2)]
        hx_read = [sem(f"hx{b}_read") for b in range(2)]
        pre_t, pre_v, pre_d = sem("small_transposed"), sem("small_copied"), sem("small_prepared")
        cact_ready = sem("cact_ready")
        lam_ready = sem("lambda_ready")
        brow_ready, brow_saved = sem("bias_row_ready"), sem("bias_row_saved")
        sumsq, var_ready, rstd_ready = sem("sumsq_ready"), sem("variance_ready"), sem("rstd_ready")
        xn_ready = sem("xn_ready")
        xt_full = sem("x_transposed")
        xt_a, xt_v = sem("x_transposed_copied_act"), sem("x_transposed_copied_vec")
        h_ready = sem("h_ready")
        win_done, win_read = sem("w_in_bank_done"), sem("w_in_bank_copied")
        f_clamped, f_exp = sem("f_clamped"), sem("f_exp")
        f_split, f_log = sem("f_split"), sem("f_logs")
        b_ready = sem("cumulated_decay_ready")
        d_ready, e_ready = sem("decay_exponent_ready"), sem("decay_ready")
        z_ready = sem("decayed_operand_ready")
        g_clamped, g_exp = sem("g_clamped"), sem("g_exp")
        or_log, or_ready = sem("head_log_ready"), sem("head_rstd_ready")
        hgrn_out = sem("hgrn_group_out")
        bias_loaded = [sem(f"bias{b}_loaded") for b in range(2)]
        max_ready, p_ready, a_ready = sem("score_max_ready"), sem("probs_ready"), sem("mixed_probs_ready")
        diff_out = sem("diff_group_out")
        wout_done, wout_read = sem("w_out_bank_done"), sem("w_out_bank_read")
        res_ready = sem("residual_chunk_ready")
        wr_loaded = sem("router_loaded")
        rt_pe, rt_act, rt_dve = sem("router_pe"), sem("router_act"), sem("router_dve")
        chosen_ready = sem("experts_chosen")
        routed = sem("routed")
        m_full = [sem(f"gather{b}_full") for b in range(2)]
        m_read = [sem(f"gather{b}_read") for b in range(2)]
        sel_ready = sem("selection_ready")
        gate_done, up_done = sem("gate_done"), sem("up_done")
        gate_clamped, gate_exp = sem("gate_clamped"), sem("gate_exp")
        hid_ready = sem("hidden_ready")
        y_done, y_act, y_dve = sem("down_done"), sem("down_copied_act"), sem("down_copied_vec")
        sc_done, sc_read = sem("scatter_done"), sem("scatter_read")
        fn_loaded = sem("final_norm_loaded")
        moe_out = sem("moe_out")
        out_ready, out_saved = sem("out_ready"), sem("out_saved")
        c_dve, c_pool, c_rounds = sem("vector_steps"), sem("gpsimd_steps"), sem("vector_round_steps")

        block = ctx.enter_context(nc.Block())

        ADA0 = 4
        WIN_G, WIN_A = 3 * GH + NT, 2 * GH + NT
        WIN_ALL = NG * (WIN_G + WIN_A)
        AUX_G = 8
        AUX_A = AUX_G + 6 * NG
        AUX_O = AUX_A + 9 * NG
        HX_G = [11, 10]
        HX_A = 6
        hx_base = [NG * n for n in HX_G]

        def w_rows(w, row, col):
            return w[row:row + 8 * P, bass.ds(col, PANEL)].rearrange("(k p) n -> p k n", p=P)

        GIVEN = 1
        given = [free[0], free[2], ada_a, ada_b, win_done, win_read, ada_copied, aux_read, hgrn_out, diff_out,
                 hid_ready, sc_read] + hx_read + m_read

        @block.sync
        def _(sp):
            for signal in given:
                sp.sem_inc(signal, GIVEN)
            for m in range(NT):
                sp.dma_start(res[:, m, :], x[m * P:(m + 1) * P, :]).then_inc(s_x, 16)

            def load(w, s, half, col, row=None):
                sp.dma_start(panelv(s), w_rows(w, (half if row is None else row) * 8 * P, col)).then_inc(full[s], 16)

            with sp.Fori(0, ADA0) as i:
                for pair, done in ((0, ada_a), (1, ada_b)):
                    col = (2 * i + pair) * PANEL
                    sp.wait_ge(free[2 * pair], GIVEN + i)
                    load(w_ada, 2 * pair, 0, col)
                    sp.wait_ge(done, GIVEN + i)
                    load(w_ada, 2 * pair + 1, 1, col)
            with sp.Fori(0, NG) as i:
                for t, (wcol, nbanks) in enumerate(((COL_FH, 0), (COL_QH, GH), (COL_IH, 2 * GH), (COL_GH, 2 * GH + NT))):
                    n = 4 * i + t
                    sp.wait_ge(free[2], GIVEN + ADA0 + n)
                    load(w_in, 2, 0, wcol + i * PANEL)
                    if t == 0:
                        sp.wait_ge(ada_b, GIVEN + ADA0)
                    sp.wait_ge(win_done, GIVEN + WIN_G * i + nbanks)
                    load(w_in, 3, 1, wcol + i * PANEL)
            with sp.Fori(0, NG) as j:
                for t, (wcol, nbanks) in enumerate(((COL_QD, 0), (COL_KD, GH), (COL_VD, 2 * GH))):
                    n = ADA0 + 4 * NG + 3 * j + t
                    sp.wait_ge(free[2], GIVEN + n)
                    load(w_in, 2, 0, wcol + j * PANEL)
                    sp.wait_ge(win_done, GIVEN + WIN_G * NG + WIN_A * j + nbanks)
                    load(w_in, 3, 1, wcol + j * PANEL)
            n = ADA0 + 4 * NG + 3 * NG
            for t in range(2):
                sp.wait_ge(free[2], GIVEN + n + t)
                load(w_out, 2, 1, t * PANEL)
                if t == 0:
                    sp.wait_ge(win_done, GIVEN + WIN_ALL)
                else:
                    sp.wait_ge(wout_done, NT)
                load(w_out, 3, 0, t * PANEL)
            sp.wait_ge(free[0], GIVEN + n + 2)
            load(w_out, 0, 1, 2 * PANEL)
            sp.wait_ge(ada_a, GIVEN + n + 2)
            load(w_out, 1, 0, 2 * PANEL)
            sp.wait_ge(free[2], GIVEN + n + 2)
            load(w_out, 2, 1, 3 * PANEL)
            sp.wait_ge(wout_done, 2 * NT)
            load(w_out, 3, 0, 3 * PANEL)

            def expert_loads(n, e, first):
                def pick(w, a, rows):
                    return w[bass.ds(e + a, 1), rows, :].rearrange("o p n -> (o p) n")

                kin = lambda w, q, a: pick(w, a, slice(q * 4 * P, (q + 1) * 4 * P)).rearrange("(k p) n -> p k n", p=P)
                dst = lambda s, a: ring[:, s, :].rearrange("p (e k n) -> p e k n", e=2, k=4)[:, a]
                kdn = lambda q, a: pick(w_down, a, slice(q * P, (q + 1) * P))
                dsd = lambda s, a: ring[:, s, :].rearrange("p (e n) -> p e n", e=2)[:, a]
                plan = [(w_gate, 0, 0, efree[0], 2 * n), (w_gate, 1, 1, efree[1], n), (w_gate, 2, 2, efree[2], 2 * n),
                        (w_gate, 3, 3, efree[3], n), (w_up, 0, 4, efree[4], 2 * n), (w_up, 1, 5, efree[5], n),
                        (w_up, 2, 0, efree[0], 2 * n + 1), (w_up, 3, 1, efree[1], n + 1),
                        (None, 0, 2, efree[2], 2 * n + 1), (None, 1, 3, gate_done, n + 1),
                        (None, 2, 4, efree[4], 2 * n + 1), (None, 3, 5, efree[5], n + 1)]
                for k, (w, q, s, released, value) in enumerate(plan):
                    if k == 1 and not first:
                        sp.wait_ge(up_done, n)
                    if k == 5 and not first:
                        sp.wait_ge(y_done, 4 * n)
                    if not first or value:
                        sp.wait_ge(released, value)
                    if first:
                        if k == 0:
                            sp.wait_ge(free[0], GIVEN + n_slot0)
                        if k == 1:
                            sp.wait_ge(wout_done, 3 * NT)
                        if k == 2:
                            sp.wait_ge(free[2], GIVEN + n_slot0)
                        if k == 3:
                            sp.wait_ge(wout_done, 4 * NT)
                        if k == 4:
                            sp.wait_ge(diff_out, GIVEN + NG)
                        if k == 5:
                            sp.wait_ge(routed, 1)
                    for a in range(2):
                        if w is None:
                            sp.dma_start(dsd(s, a), kdn(q, a)).then_inc(efull[s], 16)
                        else:
                            sp.dma_start(dst(s, a), kin(w, q, a)).then_inc(efull[s], 16)

            n_slot0 = ADA0 + 4 * NG + 3 * NG + 3
            expert_loads(0, 0, True)
            with sp.Fori(1, NPAIR) as i:
                expert_loads(i, 2 * i, False)
            sp.wait_ge(routed, 1)
            most = sp.value_load(count_i[0:1, 0:1], min_val=0, max_val=SEQ)
            with sp.If(most > CAP):
                with sp.Fori(1, ROUNDS) as r:
                    with sp.Fori(0, NPAIR) as i:
                        expert_loads(r * NPAIR + i, 2 * i, False)
            for m in range(NT):
                sp.wait_ge(out_ready, m + 1)
                sp.dma_start(out[m * P:(m + 1) * P, :], res[:, m, :]).then_inc(out_saved, 16)
            sp.wait_ge(out_saved, 16 * NT)

        @block.gpsimd
        def _(pool):
            ch = Chain(pool, c_pool)
            half = nhalf[:, 0:1]
            ch.link(pool.memset(nhalf[:, :], -0.5))
            pool.wait_ge(var_ready, 1)
            pool.tensor_tensor(stat[:, 2:4], stat[:, 2:4], half.to_broadcast([P, NT]), ALU.pow).then_inc(rstd_ready, 1)
            pool.wait_ge(brow_ready, 1)
            pool.dma_start(bias_rows.ap(), work[0:2 * NH, 6656:6656 + BIAS_W]).then_inc(brow_saved, 16)

            def load_ada(n, col):
                for s, used in ((0, free[0]), (1, ada_a)):
                    pool.wait_ge(used, GIVEN + n)
                    pool.dma_start(panelv(s), w_rows(w_ada, s * 8 * P, col)).then_inc(ada_full[s], 16)

            pool.wait_ge(full[2], 16 * (ADA0 + 1))
            with pool.Fori(0, NG) as i:
                ch.enter(i, 1)
                for t in range(3):
                    load_ada(ADA0 + 4 * i + t, 3 * D + (4 * i + t) * PANEL)
                pool.wait_ge(b_ready, i + 1)
                for lv, n in enumerate(LEVELS[1:] + [P]):
                    dt = dbuf[lv % 2]
                    if lv >= 2:
                        pool.wait_ge(z_ready, 8 * i + lv - 1)
                    if n < P:
                        b4 = bh.rearrange("p (q s n) -> p q s n", s=2, n=n)
                        d4 = dt.rearrange("p (q s n) -> p q s n", s=2, n=n)
                        ref = b4[:, :, 0, n - 1:n].to_broadcast([P, GH * SEQ // (2 * n), n])
                        if n < CHUNK:
                            pool.tensor_tensor(d4[:, :, 0, :], ref, b4[:, :, 0, :], ALU.subtract)
                            pool.tensor_tensor(d4[:, :, 1, :], b4[:, :, 1, :], ref, ALU.subtract).then_inc(d_ready, 1)
                        else:
                            pool.tensor_tensor(d4[:, :, 0, :], ref, b4[:, :, 0, :], ALU.subtract).then_inc(d_ready, 1)
                    else:
                        b4 = bh.rearrange("p (h c n) -> p h c n", c=4, n=CHUNK)
                        d4 = dt.rearrange("p (h c n) -> p h c n", c=4, n=CHUNK)
                        end = [b4[:, :, q, CHUNK - 1:CHUNK].to_broadcast([P, GH, CHUNK]) for q in range(3)]
                        ch.step(pool.tensor_tensor(d4[:, :, 0, :], end[0], b4[:, :, 0, :], ALU.subtract))
                        pool.tensor_tensor(d4[:, :, 1, :], end[1], b4[:, :, 1, :], ALU.subtract)
                        pool.tensor_tensor(d4[:, :, 3, :], b4[:, :, 3, :], end[2], ALU.add)
                        ch.wait()
                        pool.tensor_tensor(d4[:, :, 0, :], d4[:, :, 0, :], end[1], ALU.add).then_inc(d_ready, 1)
                load_ada(ADA0 + 4 * i + 3, 3 * D + (4 * i + 3) * PANEL)
                ch.leave(NG)

            def load_bias(h, b):
                for col, n, at in ((0, 2 * P, 0), (P, P, 2 * P)):
                    shifted = bass.AP(tensor=bias_rows, offset=2 * h * BIAS_W + col, ap=[[1, P], [BIAS_W, 2], [1, n]])
                    pool.dma_start(bias[:, b, :, at:at + n], shifted).then_inc(bias_loaded[b], 16)

            pool.wait_ge(brow_saved, 16)
            with pool.Fori(0, NG) as j:
                for h in range(GH):
                    if h < 3:
                        load_ada(ADA0 + 4 * NG + 3 * j + h, (8 + 3 * j) * PANEL if h == 0 else (8 + h + 11 * j) * PANEL)
                    if h == 0:
                        pool.wait_ge(hgrn_out, GIVEN + NG)
                    pool.wait_ge(hx_read[1], GIVEN + hx_base[1] + HX_A * j + (h - 3 if h < 2 else h - 1))
                    load_bias(GH * j + h, h % 2)

            for t in range(2):
                load_ada(ADA0 + 7 * NG + t, (22 + t) * PANEL)
            for k in range(2, 4):
                pool.wait_ge(var_ready, k)
                pool.tensor_tensor(stat[:, 2:4], stat[:, 2:4], half.to_broadcast([P, NT]), ALU.pow).then_inc(rstd_ready, 1)

        @block.tensor
        def _(pe):
            def mm(o, lhsT, rhs, start=True, stop=True):
                return pe.matmul(o, lhsT, rhs, start=start, stop=stop)

            pe.wait_ge(s_small, 16 * 17)
            pe.wait_ge(s_const, 1)
            pe.transpose(aux[:, 0:N_ROWS], rows[:, :], ident[0:N_ROWS, 0:N_ROWS]).then_inc(pre_t, 1)
            pe.transpose(acc[:, 0:64], brows[:, :], ident[0:64, 0:64]).then_inc(pre_t, 1)
            mm(hx[1][0:2 * NH, 0:BIAS_W], relb[:, :], work[0:BUCKETS + 1, 6656 - BIAS_W:6656]).then_inc(pre_t, 1)
            pe.wait_ge(lam_ready, 1)
            mm(hx[0][:, 0:1], ones[0:1, :], lams[0:1, 4:5]).then_inc(pre_t, 1)
            pe.wait_ge(xn_ready, NT)
            for q in range(KT // 2):
                if q >= 4:
                    pe.wait_ge((xt_a, xt_v)[q % 2], (q - 4) // 2 + 1)
                for k in range(2):
                    for m in range(NT):
                        ins = pe.transpose(pw[q % 4][:, k * SEQ + m * P:k * SEQ + (m + 1) * P],
                                           xn[:, m, (2 * q + k) * P:(2 * q + k + 1) * P], ident)
                ins.then_inc(xt_full, 1)
            pe.wait_ge(cact_ready, 1)
            pe.wait_ge(pre_v, 6)
            pe.wait_ge(brow_ready, 1)

            def ada(n, s, filled, done):
                pe.wait_ge(ada_copied, GIVEN + n)
                for half in range(2):
                    pe.wait_ge(full[s + half], filled)
                    for k in range(8):
                        q = k % 4
                        ins = mm(acc[32 * q:32 * q + 32, :], cact[:, 8 * half + k, :], panelv(s + half)[:, k, :],
                                 start=half == 0 and k < 4, stop=half == 1 and k >= 4)
                    ins.then_inc(done if half else free[s], 1)

            def ada_columns(row, use):
                pe.wait_ge(aux_read, GIVEN + use)
                for q in range(4):
                    ins = pe.transpose(aux[:, q * P:(q + 1) * P], arow[row][:, q * P:(q + 1) * P], ident)
                ins.then_inc(aux_full, 1)

            def ada_spread(row, use):
                pe.wait_ge(aux_read, GIVEN + use)
                mm(aux[:, :], ones[:, :], arow[row]).then_inc(aux_full, 1)

            def project_T(filled, banks, hooks):
                for half in range(2):
                    pe.wait_ge(full[2 + half], filled)
                    wp = panelv(2 + half)
                    order = [(k, b) for k in range(8) for b in range(GH)] if half == 0 else \
                            [(k, b) for b in range(GH) for k in range(8)]
                    for at, (k, b) in enumerate(order):
                        if half == 0 and k == 0:
                            pe.wait_ge(win_read, GIVEN + banks[b])
                        ins = mm(pw[b][:, 0:SEQ], wp[:, k, b * P:(b + 1) * P], hT[:, 8 * half + k, :],
                                 start=half == 0 and k == 0, stop=half == 1 and k == 7)
                        if half and k == 7:
                            ins.then_inc(win_done, 1)
                        elif half == 0 and at == len(order) - 1:
                            ins.then_inc(free[2], 1)
                        if at % 8 == 7 and hooks:
                            hooks.pop(0)()
                for hook in hooks:
                    hook()

            def project(filled, banks, hooks):
                for half in range(2):
                    pe.wait_ge(full[2 + half], filled)
                    wp = panelv(2 + half)
                    order = [(k, m) for k in range(8) for m in range(NT)] if half == 0 else \
                            [(k, m) for m in range(NT) for k in range(8)]
                    for at, (k, m) in enumerate(order):
                        if half == 0 and k == 0:
                            pe.wait_ge(win_read, GIVEN + banks[m])
                        ins = mm(pw[m][:, :], hT[:, 8 * half + k, m * P:(m + 1) * P], wp[:, k, :],
                                 start=half == 0 and k == 0, stop=half == 1 and k == 7)
                        if half and k == 7:
                            ins.then_inc(win_done, 1)
                        elif half == 0 and at == len(order) - 1:
                            ins.then_inc(free[2], 1)
                        if at % 4 == 3 and hooks:
                            hooks.pop(0)()
                for hook in hooks:
                    hook()

            def norm_sums(outs, use, square):
                for q in range(2):
                    for b in range(2):
                        pe.wait_ge(hx_read[b], GIVEN + outs[b] + q + 1)
                    pe.wait_ge(aux_read, GIVEN + use + q)
                    for h in range(2):
                        ins = mm(aux[:, h * SEQ:(h + 1) * SEQ], mean_w[:, :], square[:, (2 * q + h) * SEQ:(2 * q + h + 1) * SEQ])
                    ins.then_inc(aux_full, 1)

            with pe.Fori(0, ADA0) as i:
                for t, (s, done) in enumerate(((0, ada_a), (2, ada_b))):
                    ada(2 * i + t, s, 16 * i + 16, done)
                    pe.wait_ge(ada_copied, GIVEN + 2 * i + t + 1)
                    ada_columns(0, 2 * i + t)
            pe.wait_ge(h_ready, 1)

            def level(i, lv):
                z = zbuf[(lv - 1) % 2]
                if lv == 0:
                    pe.wait_ge(win_read, GIVEN + WIN_G * i + 2 * GH)
                else:
                    pe.wait_ge(z_ready, 8 * i + lv)
                for b in range(2):
                    pe.wait_ge(hx_read[b], GIVEN + HX_G[b] * i + lv)
                    for h in range(2):
                        for m in range(NT):
                            at = (2 * b + h) * SEQ + m * P
                            o = hx[b][:, h * SEQ + m * P:h * SEQ + (m + 1) * P]
                            ins = mm(o, (kh if lv == 0 else z)[:, at:at + P], (qh if lv == 0 else z)[:, at:at + P])
                    ins.then_inc(hx_full[b], 1)

            def level_across(i):
                z = zbuf[1]
                pe.wait_ge(z_ready, 8 * i + 8)
                pe.wait_ge(hx_read[0], GIVEN + HX_G[0] * i + 8)
                for h in range(GH):
                    ins = mm(hx[0][:, h * P:(h + 1) * P], z[:, h * SEQ:h * SEQ + P], z[:, h * SEQ + P:(h + 1) * SEQ])
                ins.then_inc(hx_full[0], 1)

            with pe.Fori(0, NG) as i:
                w0 = WIN_G * i
                panels = [[w0] * 4, [w0 + b + 1 for b in range(4)], [w0 + GH + b + 1 for b in range(NT)],
                          [w0 + 2 * GH + b + 1 for b in range(NT)] + [w0 + GH + b + 1 for b in range(NT, 4)]]
                u0 = AUX_G + 6 * i

                def turn_ada(t, use):
                    pe.wait_ge(ada_a, GIVEN + ADA0 + 4 * i + t + 1)
                    ada_columns(t % 2, use)

                def outputs(h):
                    b = h % 2
                    if h == 0:
                        pe.wait_ge(win_read, GIVEN + w0 + 2 * GH + NT)
                    pe.wait_ge(hx_read[b], GIVEN + HX_G[b] * i + 9 - b + h // 2)
                    o = hx[b]
                    vv = toks(vh)[:, :, h * HD:(h + 1) * HD]
                    mm(o[:, 0:P], vv[:, 0, :], sc_diag[:, h * SEQ:h * SEQ + P])
                    mm(o[:, P:SEQ], vv[:, 0, :], sc_off[:, h * P:(h + 1) * P], stop=False)
                    mm(o[:, P:SEQ], vv[:, 1, :], sc_diag[:, h * SEQ + P:(h + 1) * SEQ], start=False).then_inc(hx_full[b], 1)

                nop = lambda: None
                levels = [lambda lv=lv: level(i, lv) for lv in range(8)]
                beside = [[], [nop, lambda: turn_ada(0, u0)],
                          [nop, nop, nop, lambda: turn_ada(1, u0 + 1)] + levels[0:4],
                          levels[4:8] + [lambda: (level_across(i), turn_ada(2, u0 + 2)),
                                         lambda: (outputs(0), outputs(1)), lambda: (outputs(2), outputs(3))]]
                for t in range(4):
                    (project if t == 2 else project_T)(16 * (ADA0 + 4 * i + t + 1), panels[t], beside[t])
                norm_sums([HX_G[b] * i + 9 - b for b in range(2)], u0 + 3, zbuf[0])
                turn_ada(3, u0 + 5)

            def scores(j, h):
                for s in range(2):
                    pe.wait_ge(hx_read[s], GIVEN + hx_base[s] + HX_A * j + h)
                for s in range(2):
                    r = slice(s * QK, (s + 1) * QK)
                    q, k = heads(qd)[r, h, :], heads(kd)[r, h, :]
                    mm(hx[s][:, 0:SEQ], q[:, P:SEQ], k)
                    mm(hx[s][:, SEQ:SEQ + P], q[:, 0:P], k[:, 0:P]).then_inc(hx_full[s], 1)

            def probs_T(j, h, use):
                pe.wait_ge(a_ready, GH * j + h + 1)
                pe.wait_ge(aux_read, GIVEN + use)
                for at, col in ((0, 2 * P), (P, 0), (2 * P, P)):
                    ins = pe.transpose(aux[:, at:at + P], amix[:, col:col + P], ident)
                ins.then_inc(aux_full, 1)

            with pe.Fori(0, NG) as j:
                w0 = WIN_G * NG + WIN_A * j
                a0 = AUX_A + 9 * j
                panels = [[w0] * 4, [w0 + b + 1 for b in range(4)], [w0 + GH + b + 1 for b in range(NT)]]

                def turn_ada(t, use):
                    pe.wait_ge(ada_a, GIVEN + ADA0 + 4 * NG + 3 * j + t + 1)
                    ada_spread(t % 2, use)

                for t in range(3):
                    filled = 16 * (ADA0 + 4 * NG + 3 * j + t + 1)
                    if t == 0:
                        project_T(filled, panels[t], [])
                    elif t == 1:
                        project_T(filled, panels[t], [lambda t=t: turn_ada(t, a0 + t) for t in range(2)])
                    else:
                        nop = lambda: None
                        pe.wait_ge(win_read, GIVEN + w0 + 2 * GH)
                        scores(j, 0)
                        project(filled, panels[t], [
                            lambda: turn_ada(2, a0 + 2), nop, lambda: (probs_T(j, 0, a0 + 3), scores(j, 1)), nop,
                            lambda: (probs_T(j, 1, a0 + 4), scores(j, 2)), nop,
                            lambda: (probs_T(j, 2, a0 + 5), scores(j, 3))])
                        probs_T(j, 3, a0 + 6)
                pe.wait_ge(win_read, GIVEN + w0 + WIN_A)
                for h in range(GH):
                    b = h % 2
                    pe.wait_ge(aux_read, GIVEN + a0 + 4 + h)
                    pe.wait_ge(hx_read[b], GIVEN + hx_base[b] + HX_A * j + 4 + h // 2)
                    vv = toks(vd)[:, :, h * HD:(h + 1) * HD]
                    o = hx[b]
                    mm(o[:, 0:P], vv[:, 0, :], aT[:, h, 0:P])
                    mm(o[:, P:SEQ], vv[:, 0, :], aT[:, h, P:2 * P], stop=False)
                    mm(o[:, P:SEQ], vv[:, 1, :], aT[:, h, 2 * P:3 * P], start=False).then_inc(hx_full[b], 1)
                norm_sums([hx_base[b] + HX_A * j + 4 for b in range(2)], a0 + 7, osq_d)

            def out_project(n, s, filled, read):
                pe.wait_ge(win_read, GIVEN + WIN_ALL)
                pe.wait_ge(wout_read, read)
                for half in range(2):
                    pe.wait_ge(full[s + half], filled)
                    if half:
                        pe.wait_ge(diff_out, GIVEN + NG)
                    else:
                        pe.wait_ge(hgrn_out, GIVEN + NG)
                    wp = panelv(s + half)
                    order = [(k, m) for k in range(8) for m in range(NT)] if half == 0 else \
                            [(k, m) for m in range(NT) for k in range(8)]
                    for at, (k, m) in enumerate(order):
                        kk = k if half else 8 + k
                        ins = mm(pw[2 * (n % 2) + m][:, :], mixT[:, kk, m * P:(m + 1) * P], wp[:, k, :],
                                 start=half == 0 and k == 0, stop=half == 1 and k == 7)
                        if half and k == 7:
                            ins.then_inc(wout_done, 1)
                        elif half == 0 and at == len(order) - 1:
                            ins.then_inc(free[s], 1)

            used = ADA0 + 7 * NG
            for t in range(2):
                out_project(t, 2, 16 * (used + t + 1), 0)
                pe.wait_ge(ada_a, GIVEN + used + t + 1)
                ada_spread(t, AUX_O + t)
            out_project(2, 0, 16 * (ADA0 + 1), 2)
            out_project(3, 2, 16 * (used + 3), 4)

            pe.wait_ge(xn_ready, 2 * NT)
            pe.wait_ge(aux_read, GIVEN + AUX_O + 2)
            pe.wait_ge(wout_read, 8)
            for q in range(KT // 2):
                for k in range(2):
                    for m in range(NT):
                        ins = pe.transpose(bank[q][:, k * SEQ + m * P:k * SEQ + (m + 1) * P],
                                           xn2[:, m, (2 * q + k) * P:(2 * q + k + 1) * P], ident)
                ins.then_inc(xt_full, 1)
            pe.wait_ge(wr_loaded, 16)
            for k in range(KT):
                q = k // 2
                pe.wait_ge((xt_a, xt_v)[q % 2], 4 + q // 2 + 1)
                ins = mm(bank[0][0:NE, 0:SEQ], wr[:, k, :], h2T[:, k, :], start=k == 0, stop=k == KT - 1)
            ins.then_inc(rt_pe, 1)
            pe.wait_ge(rt_act, 1)
            for m in range(NT):
                ins = pe.transpose(bank[1][:, m * NE:(m + 1) * NE], lt[:, m * P:(m + 1) * P], ident[0:NE, 0:NE])
            ins.then_inc(rt_pe, 1)
            pe.wait_ge(chosen_ready, 1)
            mm(bank[2][:, 0:NE], before, chosen[:, 0, :])
            mm(bank[2][:, NE:2 * NE], ones[:, :], chosen[:, 0, :], stop=False)
            mm(bank[2][:, NE:2 * NE], before, chosen[:, 1, :], start=False)
            mm(bank[2][:, 2 * NE:3 * NE], ones[:, :], chosen[:, 0, :], stop=False)
            mm(bank[2][:, 2 * NE:3 * NE], ones[:, :], chosen[:, 1, :], start=False).then_inc(rt_pe, 1)

            def experts(n, r):
                half = [slice(0, CAP), slice(CAP, P)]
                pe.wait_ge(sel_ready, n + r + 1)
                for j in range(4):
                    b = j % 2
                    pe.wait_ge(m_read[b], GIVEN + 3 * n + j // 2)
                    for kk in range(4):
                        k = 4 * j + kk
                        for m in range(NT):
                            ins = mm(hx[b][:, kk * P:(kk + 1) * P], xn2[:, m, k * P:(k + 1) * P], sel[:, m, :],
                                     start=m == 0, stop=m == NT - 1)
                    ins.then_inc(m_full[b], 1)
                pe.wait_ge(m_read[0], GIVEN + 3 * n + 2)
                for m in range(NT):
                    ins = pe.transpose(hx[0][:, m * P:(m + 1) * P], selg[:, m, :], ident)
                ins.then_inc(m_full[0], 1)
                for o, slots, fills, done in ((acc, (0, 1, 2, 3), (1, 1, 1, 1), gate_done), (aux, (4, 5, 0, 1), (1, 1, 2, 2), up_done)):
                    pe.wait_ge(hid_ready, GIVEN + n)
                    for q, (s, f) in enumerate(zip(slots, fills)):
                        pe.wait_ge(efull[s], 32 * (2 * n + f))
                        if o is acc:
                            pe.wait_ge(m_read[q % 2], GIVEN + 3 * n + q // 2 + 1)
                        wp = ring[:, s, :].rearrange("p (e k n) -> p e k n", e=2, k=4)
                        for kk in range(4):
                            k = 4 * q + kk
                            for e in range(2):
                                ins = mm(o[half[e], :], xe[:, k, half[e]], wp[:, e, kk, :], start=k == 0, stop=k == KT - 1)
                        ins.then_inc(done if q == 3 else efree[s], 1)
                pe.wait_ge(hid_ready, GIVEN + n + 1)
                pe.wait_ge(m_read[1], GIVEN + 3 * n + 2)
                for f in range(FT):
                    ins = pe.transpose(hx[1][:, f * P:(f + 1) * P], hid[:, f * P:(f + 1) * P], ident)
                ins.then_inc(m_full[1], 1)
                pe.wait_ge(m_read[1], GIVEN + 3 * n + 3)
                pe.wait_ge(sc_read, GIVEN + 8 * n)
                for f, s in enumerate((2, 3, 4, 5)):
                    pe.wait_ge(efull[s], 32 * (2 * n + 2))
                    wp = ring[:, s, :].rearrange("p (e n) -> p e n", e=2)
                    for dc in range(NP_D):
                        for e in range(2):
                            ins = mm(pw[dc][half[e], :], hidT[:, f, half[e]], wp[:, e, dc * PANEL:(dc + 1) * PANEL],
                                     start=f == 0, stop=f == FT - 1)
                        if f == FT - 1:
                            ins.then_inc(y_done, 1)
                    if f < FT - 1:
                        ins.then_inc(efree[s], 1)
                pe.wait_ge(m_read[0], GIVEN + 3 * n + 3)
                pe.wait_ge(y_act, 2 * n + 2)
                pe.wait_ge(y_dve, 2 * n + 2)
                for m in range(NT):
                    for dc in range(NP_D):
                        if m:
                            pe.wait_ge(sc_read, GIVEN + 8 * n + dc + 1)
                        mm(pw[dc][:, :], selT[:, m * P:(m + 1) * P], ys[:, dc * PANEL:(dc + 1) * PANEL]).then_inc(sc_done, 1)

            with pe.Fori(0, NPAIR) as i:
                experts(i, 0)
            pe.wait_ge(routed, 1)
            most = pe.value_load(count_i[0:1, 0:1], min_val=0, max_val=SEQ)
            with pe.If(most > CAP):
                with pe.Fori(1, ROUNDS) as r:
                    with pe.Fori(0, NPAIR) as i:
                        experts(r * NPAIR + i, r)

        @block.scalar
        def _(act):
            small = lambda dst, src: act.dma_start(dst, src).then_inc(s_small, 16)
            small(cst[:, :], consts)
            small(rows[ROW_C:ROW_AN, :], c.rearrange("o (k p) -> (o k) p", p=P))
            small(rows[ROW_AN:ROW_FN, :], attn_norm.rearrange("o (k p) -> (o k) p", p=P))
            small(rows[ROW_FN:ROW_LB, :], ffn_norm.rearrange("o (k p) -> (o k) p", p=P))
            small(rows[ROW_LB:ROW_SUB, :], hgrn_lb.rearrange("o (k p) -> (o k) p", p=P))
            small(rows[ROW_SUB:ROW_HN, :], diff_subln)
            small(rows[ROW_HN:N_ROWS, :], hgrn_norm)
            bm = b_ada.rearrange("o (k p) -> (o k) p", p=P)
            small(brows[0:2 * KT, :], bm[0:2 * KT, :])
            small(brows[2 * KT:4 * KT, :], bm[3 * KT:5 * KT, :])
            for n, v in enumerate((lambda_q1, lambda_q2, lambda_k1, lambda_k2)):
                small(lam[0:1, n, :], v)
            small(relb[0:BUCKETS, :], rel_bias)
            small(work[0:BUCKETS + 1, 6656 - BIAS_W:6656], onehot)
            small(work[:, 0:len(LEVELS) * P], masks)
            small(stat[:, 8:8 + NE], b_router.rearrange("(o e) -> o e", o=1).to_broadcast([P, NE]))
            for n, col in enumerate((2 * D, 5 * D)):
                act.dma_start(gates_bc[:, n * D:(n + 1) * D], b_ada[0:1, col:col + D].to_broadcast([P, D])).then_inc(s_bload, 16)

            act.wait_ge(s_x, 32)
            for m in range(NT):
                act.activation(xn[:, m, :], res[:, m, :], ACT.Square, accum_out=stat[:, m:m + 1]).then_inc(sumsq, 1)
            act.wait_ge(pre_t, 1)
            act.activation(cols[:, :], aux[:, 0:N_ROWS], ACT.Copy).then_inc(pre_v, 1)
            act.wait_ge(pre_v, 1)
            act.activation(stat[:, 24:24 + KT], cols[:, ROW_C:ROW_C + KT], ACT.Exp, scale=-1.0).then_inc(pre_v, 1)
            act.wait_ge(pre_t, 2)
            act.activation(bcols[:, :], acc[:, 0:64], ACT.Copy).then_inc(pre_v, 1)
            act.wait_ge(pre_t, 3)
            act.activation(work[0:2 * NH, 6656:6656 + BIAS_W], hx[1][0:2 * NH, 0:BIAS_W], ACT.Copy).then_inc(brow_ready, 1)
            act.wait_ge(pre_d, 1)
            act.activation(lams[0:1, 2:4], lams[0:1, 0:2], ACT.Exp).then_inc(pre_v, 1)
            act.wait_ge(pre_d, 2)
            act.activation(lb[:, 1, :], lb[:, 0, :], ACT.Exp).then_inc(pre_v, 1)
            act.wait_ge(pre_t, 4)
            act.activation(stat[:, 4:5], hx[0][:, 0:1], ACT.Copy, scale=-1.0).then_inc(pre_v, 1)
            for q in range(0, KT // 2, 2):
                act.wait_ge(xt_full, q + 1)
                act.activation(hT[:, 2 * q:2 * q + 2, :].rearrange("p k t -> p (k t)"), pw[q % 4][:, :], ACT.Copy).then_inc(xt_a, 1)

            def copy_row(done, value):
                act.wait_ge(done, GIVEN + value)
                act.activation(arow[0], acc[:, :], ACT.Copy).then_inc(ada_copied, 1)

            with act.Fori(0, ADA0) as i:
                copy_row(ada_a, i + 1)
                copy_row(ada_b, i + 1)

            backwards = lambda t: t.rearrange("p (c n) -> p c n", n=P)[:, :, ::-1]

            def copy_banks(w0, dst):
                for b in range(GH):
                    act.wait_ge(win_done, GIVEN + w0 + b + 1)
                    act.activation(dst[:, b * SEQ:(b + 1) * SEQ], pw[b][:, 0:SEQ], ACT.Copy).then_inc(win_read, 1)

            def copy_queries(w0, dst):
                for b in range(GH):
                    act.wait_ge(win_done, GIVEN + w0 + b + 1)
                    act.activation(dst[:, b * SEQ:(b + 1) * SEQ].rearrange("p (c n) -> p c n", n=P),
                                   backwards(pw[b][:, 0:SEQ]), ACT.Copy, scale=float(QK) ** -0.5).then_inc(win_read, 1)

            def copy_values(w0, dst):
                for m in range(NT):
                    act.wait_ge(win_done, GIVEN + w0 + m + 1)
                    act.activation(toks(dst)[:, m, :], pw[m][:, :], ACT.Copy).then_inc(win_read, 1)

            def head_outputs(used, dst, square):
                for h in range(GH):
                    b = h % 2
                    act.wait_ge(hx_full[b], used[b] + h // 2 + 1)
                    at = slice(h * SEQ, (h + 1) * SEQ)
                    act.activation(dst[:, at], hx[b][:, 0:SEQ], ACT.Copy)
                    act.activation(square[:, at], hx[b][:, 0:SEQ], ACT.Square).then_inc(hx_read[b], 1)

            def rstd(read, n, src, dst):
                act.wait_ge(aux_read, GIVEN + read)
                act.activation(dst, src, ACT.Ln).then_inc(or_log, 1)
                act.wait_ge(or_log, n + 1)
                act.activation(dst, dst, ACT.Exp, scale=-0.5).then_inc(or_ready, 1)

            with act.Fori(0, NG) as i:
                w0 = WIN_G * i
                act.wait_ge(hgrn_out, GIVEN + i)
                copy_banks(w0, dbuf[0])
                act.wait_ge(f_clamped, i + 1)
                act.activation(zbuf[0], dbuf[1], ACT.Exp, scale=-1.0).then_inc(f_exp, 1)
                act.wait_ge(f_split, i + 1)
                act.activation(zbuf[0], dbuf[1], ACT.Ln).then_inc(f_log, 1)
                act.activation(zbuf[1], dbuf[0], ACT.Ln, scale=1.0 / SPLIT).then_inc(f_log, 1)
                copy_banks(w0 + GH, qh)
                for lv, n in enumerate(LEVELS[1:] + [P]):
                    act.wait_ge(d_ready, 8 * i + lv + 1)
                    d = dbuf[lv % 2]
                    if n < CHUNK:
                        act.activation(d, d, ACT.Exp).then_inc(e_ready, 1)
                    elif n == CHUNK:
                        d4, b4 = (t.rearrange("p (q s n) -> p q s n", s=2, n=n) for t in (d, bh))
                        act.activation(d4[:, :, 0, :], d4[:, :, 0, :], ACT.Exp)
                        act.activation(d4[:, :, 1, :], b4[:, :, 1, :], ACT.Exp).then_inc(e_ready, 1)
                    else:
                        d4, b4 = (t.rearrange("p (h c n) -> p h c n", c=4, n=CHUNK) for t in (d, bh))
                        act.activation(d4[:, :, 0:2, :], d4[:, :, 0:2, :], ACT.Exp)
                        act.activation(d4[:, :, 3, :], d4[:, :, 3, :], ACT.Exp)
                        act.activation(d4[:, :, 2, :], b4[:, :, 2, :], ACT.Exp).then_inc(e_ready, 1)
                    if lv == 4:
                        copy_values(w0 + 2 * GH, vh)
                head_outputs([HX_G[b] * i + 9 - b for b in range(2)], ohb, zbuf[0])
                copy_banks(w0 + 2 * GH + NT, gh)
                act.wait_ge(g_clamped, i + 1)
                act.activation(zbuf[1], zbuf[1], ACT.Exp, scale=-1.0).then_inc(g_exp, 1)
                rstd(AUX_G + 6 * i + 5, i, dbuf[0], dbuf[1])

            act.wait_ge(hgrn_out, GIVEN + NG)
            with act.Fori(0, NG) as j:
                w0 = WIN_G * NG + WIN_A * j
                a0 = AUX_A + 9 * j
                act.wait_ge(diff_out, GIVEN + j)
                copy_queries(w0, qd)
                copy_banks(w0 + GH, kd)
                for h in range(GH):
                    act.wait_ge(max_ready, GH * j + h + 1)
                    for s in range(2):
                        for q, (at, n) in enumerate(((0, SEQ), (SEQ, P))):
                            v = sbuf[:, h % 2, s, at:at + n]
                            ins = act.activation(v, v, ACT.Exp, bias=stat[:, 44 + 2 * q + s:45 + 2 * q + s],
                                                 accum_out=stat[:, 48 + 2 * q + s:49 + 2 * q + s])
                    ins.then_inc(p_ready, 1)
                    act.wait_ge(aux_full, a0 + 4 + h)
                    act.activation(aT[:, h, :].rearrange("p (c n) -> p c n", n=P), backwards(aux[:, 0:3 * P]),
                                   ACT.Copy).then_inc(aux_read, 1)
                copy_values(w0 + 2 * GH, vd)
                act.wait_ge(a_ready, GH * j + GH)
                head_outputs([hx_base[b] + HX_A * j + 4 for b in range(2)], odb, osq_d)
                rstd(a0 + 9, NG + j, rs_d, rs_d)

            act.wait_ge(diff_out, GIVEN + NG)
            act.dma_start(wr, w_router.rearrange("(k p) e -> p k e", p=P)).then_inc(wr_loaded, 16)
            for q in range(NT * NP_D):
                n, m = q // NT, q % NT
                act.wait_ge(res_ready, q + 1)
                act.activation(work[:, q * PANEL:(q + 1) * PANEL], res[:, m, n * PANEL:(n + 1) * PANEL], ACT.Square,
                               accum_out=stat[:, 52 + m * NP_D + n:53 + m * NP_D + n]).then_inc(sumsq, 1)
            for q in range(0, KT // 2, 2):
                act.wait_ge(xt_full, KT // 2 + q + 1)
                for k in (2 * q, 2 * q + 1):
                    ins = act.activation(h2T[:, k, :], bank[q][:, (k % 2) * SEQ:(k % 2 + 1) * SEQ], ACT.Identity,
                                         scale=a_mul[:, KT + k:KT + k + 1], bias=mod[:, 2 * KT + k:2 * KT + k + 1])
                ins.then_inc(xt_a, 1)
            act.wait_ge(wout_read, NT * NP_D)
            act.dma_start(fnorm, final_norm.rearrange("(o d) -> o d", o=1).to_broadcast([P, D])).then_inc(fn_loaded, 16)
            act.wait_ge(rt_pe, 1)
            act.activation(lt, bank[0][0:NE, 0:SEQ], ACT.Copy).then_inc(rt_act, 1)
            act.wait_ge(rt_dve, 1)
            act.activation(prob, prob, ACT.Exp).then_inc(rt_act, 1)

            def experts(n):
                for j in (0, 2):
                    act.wait_ge(m_full[0], 3 * n + j // 2 + 1)
                    for kk in range(4):
                        k = 4 * j + kk
                        ins = act.activation(xe[:, k, :], hx[0][:, kk * P:(kk + 1) * P], ACT.Identity,
                                             scale=a_mul[:, KT + k:KT + k + 1], bias=mod[:, 2 * KT + k:2 * KT + k + 1])
                    ins.then_inc(m_read[0], 1)
                act.wait_ge(m_full[0], 3 * n + 3)
                act.activation(selT, hx[0][:, 0:SEQ], ACT.Copy).then_inc(m_read[0], 1)
                act.wait_ge(gate_clamped, n + 1)
                act.activation(hid, hid, ACT.Exp, scale=-1.0).then_inc(gate_exp, 1)
                act.wait_ge(m_full[1], 3 * n + 3)
                act.activation(hidT[:, :, :], hx[1][:, :].rearrange("p (f s) -> p f s", f=FT), ACT.Copy).then_inc(m_read[1], 1)
                for dc in range(2):
                    act.wait_ge(y_done, 4 * n + dc + 1)
                    act.activation(ys[:, dc * PANEL:(dc + 1) * PANEL], pw[dc][:, :], ACT.Copy).then_inc(y_act, 1)

            with act.Fori(0, NPAIR) as i:
                experts(i)
            act.wait_ge(routed, 1)
            most = act.value_load(count_i[0:1, 0:1], min_val=0, max_val=SEQ)
            with act.If(most > CAP):
                with act.Fori(1, ROUNDS) as r:
                    with act.Fori(0, NPAIR) as i:
                        experts(r * NPAIR + i)
            act.wait_ge(moe_out, 1)
            for m in range(NT):
                act.activation(xn2[:, m, :], res[:, m, :], ACT.Square, accum_out=stat[:, m:m + 1]).then_inc(sumsq, 1)

        @block.vector
        def _(dve):
            ch = Chain(dve, c_dve)
            tt, ts, stt = dve.tensor_tensor, dve.tensor_scalar, dve.scalar_tensor_tensor
            dve.memset(ones[:, :], 1.0)
            dve.memset(mean_w[:, :], 1.0 / HD)
            dve.memset(cact[:, :, :], 0.0)
            dve.memset(sc_diag, 0.0)
            dve.memset(pos[:, :, :], -1.0)
            dve.memset(gate[:, :, :], 0.0)
            dve.memset(relb[BUCKETS:BUCKETS + 1, :], 1.0)
            ch.link(dve.memset(resets[:, :], 1.0))
            dve.memset(resets[:, 0:SEQ:CHUNK], 0.0).then_inc(s_const, 1)
            dve.wait_ge(s_const, 1)
            dve.wait_ge(sumsq, NT)
            ts(stat[:, 2:4], stat[:, 0:2], 1.0 / D, EPS, ALU.mult, ALU.add).then_inc(var_ready, 1)
            dve.wait_ge(s_small, 16 * 17)
            dve.tensor_copy(msk[:, :, :].rearrange("p l n -> p (l n)"), work[:, 0:len(LEVELS) * P]).then_inc(mask_ready, 1)
            ch.link(tt(lam[0:1, 0:2, :], lam[0:1, 0:2, :], lam[0:1, 2:4, :], ALU.mult))
            dve.reduce_sum(lams[0:1, 0:2], lam[0:1, 0:2, :], axis=AX).then_inc(pre_d, 1)
            dve.wait_ge(rstd_ready, 1)
            for m in range(NT):
                ts(xn[:, m, :], res[:, m, :], stat[:, 2 + m:3 + m], None, ALU.mult).then_inc(xn_ready, 1)
            dve.wait_ge(pre_v, 1)
            lbc = cols[:, ROW_LB:ROW_LB + NH]
            tt(lb[:, 0, :], lbc, lbc, ALU.subtract).then_inc(pre_d, 1)
            dve.wait_ge(pre_v, 2)
            ch.link(ts(stat[:, 24:24 + KT], stat[:, 24:24 + KT], 1.0, None, ALU.add))
            ch.link(dve.reciprocal(stat[:, 24:24 + KT], stat[:, 24:24 + KT]))
            ch.link(tt(ccol[:, :], stat[:, 24:24 + KT], cols[:, ROW_C:ROW_C + KT], ALU.mult))
            dve.tensor_copy(cact[:, :, 0], ccol[:, :]).then_inc(cact_ready, 1)
            dve.wait_ge(pre_v, 4)
            stt(lams[0:1, 4:5], lams[0:1, 2:3], LAMBDA_INIT, lams[0:1, 3:4], ALU.add, ALU.subtract).then_inc(lam_ready, 1)
            dve.wait_ge(pre_v, 5)
            ch.link(dve.reciprocal(lb[:, 2, :], lb[:, 1, :]))
            ch.link(tt(lb[:, 3, :], lb[:, 1, :], lb[:, 2, :], ALU.mult))
            ch.link(tt(lb[:, 4, :], lb[:, 3, :], lb[:, 3, :], ALU.subtract))
            ch.link(ts(lb[:, 4, :], lb[:, 4, :], 0.0, None, ALU.max))
            ch.step(ts(lb[:, 0, :], lb[:, 4, :], -1.0, 1.0, ALU.mult, ALU.add))
            ch.link(ts(cols[:, ROW_SUB:ROW_SUB + 1], cols[:, ROW_SUB:ROW_SUB + 1], 1.0 - LAMBDA_INIT, None, ALU.mult))
            for q in range(1, KT // 2, 2):
                dve.wait_ge(xt_full, q + 1)
                dve.tensor_copy(hT[:, 2 * q:2 * q + 2, :].rearrange("p k t -> p (k t)"), pw[q % 4][:, :]).then_inc(xt_v, 1)

            def sum_columns(use, col):
                dve.wait_ge(aux_full, use + 1)
                part = aux[:, :].rearrange("p (q n) -> p q n", q=4)
                dve.reduce_sum(mod[:, bass.ds(col, 4)], part, axis=AX).then_inc(aux_read, 1)

            def sum_panel(n, row, posted, parts=range(4)):
                for part in parts:
                    half = part // 2
                    if part == 0:
                        dve.wait_ge(aux_full, posted)
                    if part % 2 == 0:
                        dve.wait_ge(ada_full[half], 16 * (n - ADA0 + 1))
                    for k in range(part % 2 * 4, part % 2 * 4 + 4):
                        kk = 8 * half + k
                        if kk == 0:
                            ins = ts(arow[row], panelv(half)[:, k, :], ccol[:, kk:kk + 1], None, ALU.mult)
                        else:
                            ins = stt(arow[row], panelv(half)[:, k, :], ccol[:, kk:kk + 1], arow[row], ALU.mult, ALU.add)
                        if k < 7:
                            ch.link(ins)
                        elif half == 0:
                            ins.then_inc(free[0], 1)
                            dve.wait_ge(free[0], GIVEN + n + 1)
                        else:
                            ins.then_inc(ada_a, 1)

            with dve.Fori(0, ADA0) as i:
                for t in range(2):
                    sum_columns(2 * i + t, 8 * i + 4 * t)
            dve.wait_ge(aux_read, GIVEN + AUX_G)
            dve.wait_ge(pre_v, 3)
            ch.link(tt(mod[:, 0:2 * KT], mod[:, 0:2 * KT], bcols[:, 0:2 * KT], ALU.add))
            ch.link(stt(a_mul[:, 0:KT], mod[:, KT:2 * KT], 1.0, cols[:, ROW_AN:ROW_AN + KT], ALU.add, ALU.mult))
            dve.wait_ge(xt_a, KT // 4)
            dve.wait_ge(xt_v, KT // 4)
            for k in range(KT):
                ins = ts(hT[:, k, :], hT[:, k, :], a_mul[:, k:k + 1], mod[:, k:k + 1], ALU.mult, ALU.add)
            ins.then_inc(h_ready, 1)

            dve.wait_ge(brow_saved, 16)
            with dve.Fori(0, NG) as i:
                ch.enter(i, PER_HGRN)
                w0 = WIN_G * i
                u0 = AUX_G + 6 * i
                n0 = ADA0 + 4 * i
                sum_panel(n0, 0, u0 - 3)
                dve.wait_ge(win_read, GIVEN + w0 + GH)
                ts(dbuf[1], dbuf[0], -CLAMP, CLAMP, ALU.max, ALU.min).then_inc(f_clamped, 1)
                sum_columns(u0, 2 * KT + 16 * i)
                dve.wait_ge(f_exp, i + 1)
                ch.link(ts(zbuf[1], zbuf[0], 1.0, None, ALU.add))
                ch.link(dve.reciprocal(zbuf[1], zbuf[1]))
                for h in range(GH):
                    hd = i * GH + h
                    at = slice(h * SEQ, (h + 1) * SEQ)
                    stt(kh[:, at], zbuf[0][:, at], lb[:, 0, bass.ds(hd, 1)], zbuf[1][:, at], ALU.mult, ALU.mult)
                    ch.step(ts(dbuf[0][:, at], zbuf[1][:, at], lb[:, 0, bass.ds(hd, 1)], lb[:, 4, bass.ds(hd, 1)], ALU.mult, ALU.add))
                ch.wait()
                ts(dbuf[1], dbuf[0], SPLIT, None, ALU.max)
                ts(dbuf[0], dbuf[0], TINY, SPLIT, ALU.max, ALU.min).then_inc(f_split, 1)
                dve.wait_ge(f_log, 2 * i + 2)
                ch.link(tt(dbuf[0], zbuf[0], zbuf[1], ALU.add))
                for h in range(GH):
                    at = slice(h * SEQ, (h + 1) * SEQ)
                    ins = dve.tensor_tensor_scan(bh[:, at], resets[:, :], dbuf[0][:, at], 0.0, ALU.mult, ALU.add)
                ins.then_inc(b_ready, 1)
                sum_panel(n0 + 1, 1, u0)

                def decay(lv, n):
                    dve.wait_ge(e_ready, 8 * i + lv + 1)
                    z4, d4, k4, q4 = (t.rearrange("p (q s n) -> p q s n", s=2, n=n) for t in (zbuf[lv % 2], dbuf[lv % 2], kh, qh))
                    tt(z4[:, :, 0, :], k4[:, :, 0, :], d4[:, :, 0, :], ALU.mult)
                    tt(z4[:, :, 1, :], q4[:, :, 1, :], d4[:, :, 1, :], ALU.mult).then_inc(z_ready, 1)

                def keep(level):
                    for b in range(2):
                        dve.wait_ge(hx_full[b], HX_G[b] * i + level + 1)
                        dst = sc_diag[:, b * 4 * P:(b + 1) * 4 * P].rearrange("p (q n) -> p q n", n=P)
                        ch.step(dve.memset(waiter[:, 2 * level + b:2 * level + b + 1], 0.0))
                        own = msk[:, level:level + 1, :].to_broadcast([P, 4, P])
                        dve.copy_predicated(dst, own, hx[b][:, :].rearrange("p (q n) -> p q n", n=P)).then_inc(hx_read[b], 1)

                halves = LEVELS[1:] + [P]
                dve.wait_ge(mask_ready, 1)
                dve.wait_ge(win_read, GIVEN + w0 + 2 * GH)
                decay(0, halves[0])
                decay(1, halves[1])
                sum_columns(u0 + 1, 2 * KT + 16 * i + 4)
                keep(0)
                for level in range(1, 8):
                    keep(level)
                    if level + 1 < 8:
                        decay(level + 1, halves[level + 1])
                    if level < 5:
                        sum_panel(n0 + 2, 0, u0 + 1, [level - 1])
                dve.wait_ge(hx_full[0], HX_G[0] * i + 9)
                dve.tensor_copy(sc_off, hx[0][:, :]).then_inc(hx_read[0], 1)
                sum_columns(u0 + 2, 2 * KT + 16 * i + 8)
                sum_panel(n0 + 3, 1, u0 + 2)
                for q in range(2):
                    dve.wait_ge(aux_full, u0 + 4 + q)
                    ts(dbuf[0][:, q * PANEL:(q + 1) * PANEL], aux[:, :], EPS, None, ALU.add).then_inc(aux_read, 1)
                dve.wait_ge(win_read, GIVEN + w0 + WIN_G)
                ts(zbuf[1], gh, -CLAMP, None, ALU.max).then_inc(g_clamped, 1)
                sum_columns(u0 + 5, 2 * KT + 16 * i + 12)
                dve.wait_ge(g_exp, i + 1)
                ch.link(ts(zbuf[1], zbuf[1], 1.0, None, ALU.add))
                ch.link(dve.reciprocal(zbuf[1], zbuf[1]))
                ch.link(stt(gh, gh, cols[:, ROW_HN:ROW_HN + 1], zbuf[1], ALU.mult, ALU.mult))
                dve.wait_ge(or_ready, i + 1)
                for b in range(2):
                    dve.wait_ge(hx_read[b], GIVEN + HX_G[b] * (i + 1))
                ch.link(tt(ohb, ohb, dbuf[1], ALU.mult))
                tt(mixT[:, bass.ds(NH + GH * i, GH), :].rearrange("p h t -> p (h t)"), ohb, gh, ALU.mult).then_inc(hgrn_out, 1)
                ch.leave(NG)

            dve.wait_ge(s_bload, 32)

            def add_gate(use, col):
                dve.wait_ge(aux_full, use + 1)
                g = gates_bc[:, bass.ds(col, PANEL)]
                tt(g, aux[:, :], g, ALU.add).then_inc(aux_read, 1)

            with dve.Fori(0, NG) as j:
                ch.enter(j, PER_DIFF)
                a0 = AUX_A + 9 * j
                n0 = ADA0 + 4 * NG + 3 * j
                sum_panel(n0, 0, a0)
                sum_panel(n0 + 1, 1, a0)
                add_gate(a0, 3 * j * PANEL)
                add_gate(a0 + 1, (3 * j + 1) * PANEL)
                sum_panel(n0 + 2, 0, a0 + 1)
                for h in range(GH):
                    b = h % 2
                    dve.wait_ge(bias_loaded[b], 64 * j + 32 * (h // 2 + 1))
                    for s in range(2):
                        dve.wait_ge(hx_full[s], hx_base[s] + HX_A * j + h + 1)
                        tt(sbuf[:, b, s, :], hx[s][:, 0:3 * P], bias[:, b, s, :], ALU.add).then_inc(hx_read[s], 1)
                    for s in range(2):
                        dve.wait_ge(hx_read[s], GIVEN + hx_base[s] + HX_A * j + h + 1)
                    ch.step(dve.reduce_max(stat[:, 44:46], sbuf[:, b, :, 0:SEQ], axis=AX))
                    ch.link(dve.reduce_max(stat[:, 46:48], sbuf[:, b, :, SEQ:3 * P], axis=AX))
                    ts(stat[:, 44:48], stat[:, 44:48], -1.0, None, ALU.mult).then_inc(max_ready, 1)
                    if h == 0:
                        add_gate(a0 + 2, (3 * j + 2) * PANEL)
                    dve.wait_ge(p_ready, GH * j + h + 1)
                    ch.link(dve.reciprocal(stat[:, 48:52], stat[:, 48:52]))
                    ch.link(ts(stat[:, 49:52:2], stat[:, 49:52:2], stat[:, 4:5], None, ALU.mult))
                    if h:
                        dve.wait_ge(aux_full, a0 + 3 + h)
                    for q, (at, n) in enumerate(((0, SEQ), (SEQ, P))):
                        ch.step(ts(amix[:, at:at + n], sbuf[:, b, 1, at:at + n], stat[:, 49 + 2 * q:50 + 2 * q], None, ALU.mult))
                    ch.wait()
                    for q, (at, n) in enumerate(((0, SEQ), (SEQ, P))):
                        ins = stt(amix[:, at:at + n], sbuf[:, b, 0, at:at + n], stat[:, 48 + 2 * q:49 + 2 * q],
                                  amix[:, at:at + n], ALU.mult, ALU.add)
                    ins.then_inc(a_ready, 1)
                for q in range(2):
                    dve.wait_ge(aux_full, a0 + 8 + q)
                    ts(rs_d[:, q * PANEL:(q + 1) * PANEL], aux[:, :], EPS, None, ALU.add).then_inc(aux_read, 1)
                dve.wait_ge(or_ready, NG + j + 1)
                for b in range(2):
                    dve.wait_ge(hx_read[b], GIVEN + hx_base[b] + HX_A * (j + 1))
                stt(mixT[:, bass.ds(GH * j, GH), :].rearrange("p h t -> p (h t)"), odb, cols[:, ROW_SUB:ROW_SUB + 1],
                    rs_d, ALU.mult, ALU.mult).then_inc(diff_out, 1)
                ch.leave(NG)

            ch.link(tt(mod[:, 2 * KT:4 * KT], mod[:, 2 * KT:4 * KT], bcols[:, 2 * KT:4 * KT], ALU.add))
            ch.link(stt(a_mul[:, KT:2 * KT], mod[:, 3 * KT:4 * KT], 1.0, cols[:, ROW_FN:ROW_FN + KT], ALU.add, ALU.mult))
            for t in range(2):
                sum_panel(ADA0 + 7 * NG + t, t, AUX_O)
            for q in range(NT * NP_D):
                n, m = q // NT, q % NT
                at = slice(n * PANEL, (n + 1) * PANEL)
                dve.wait_ge(wout_done, q + 1)
                if q:
                    dve.wait_ge(res_ready, q)
                tt(tmp, pw[2 * (n % 2) + m][:, :], gates_bc[:, at], ALU.mult).then_inc(wout_read, 1)
                dve.wait_ge(wout_read, q + 1)
                tt(res[:, m, at], res[:, m, at], tmp, ALU.add).then_inc(res_ready, 1)
                if q in (1, 3):
                    add_gate(AUX_O + q // 2, (6 + q // 2) * PANEL)
            dve.wait_ge(sumsq, NT + NT * NP_D)
            ch.link(dve.reduce_sum(stat[:, 0:2], stat[:, 52:60].rearrange("p (m n) -> p m n", m=NT), axis=AX))
            ts(stat[:, 2:4], stat[:, 0:2], 1.0 / D, EPS, ALU.mult, ALU.add).then_inc(var_ready, 1)
            dve.wait_ge(rstd_ready, 2)
            dve.wait_ge(res_ready, NT * NP_D)
            for m in range(NT):
                ts(xn2[:, m, :], res[:, m, :], stat[:, 2 + m:3 + m], None, ALU.mult).then_inc(xn_ready, 1)
            for q in range(1, KT // 2, 2):
                dve.wait_ge(xt_full, KT // 2 + q + 1)
                for k in (2 * q, 2 * q + 1):
                    ins = ts(h2T[:, k, :], bank[q][:, (k % 2) * SEQ:(k % 2 + 1) * SEQ], a_mul[:, KT + k:KT + k + 1],
                             mod[:, 2 * KT + k:2 * KT + k + 1], ALU.mult, ALU.add)
                ins.then_inc(xt_v, 1)

            spread = lambda v, w: v.rearrange("p (m o) -> p m o", o=1).to_broadcast([P, v.shape[1], w])
            m2 = rview(352, 2)
            v1, v2, rs = rview(354, 2), rview(356, 2), rview(358, 2)
            gm = rview(360, 2)
            dve.wait_ge(rt_pe, 2)
            br = stat[:, 8:8 + NE].rearrange("p (o e) -> p o e", o=1).to_broadcast([P, NT, NE])
            ch.link(tt(logit, bank[1][:, 0:NT * NE].rearrange("p (m e) -> p m e", m=NT), br, ALU.add))
            ch.link(dve.reduce_max(m2, logit, axis=AX))
            tt(prob, logit, spread(m2, NE), ALU.subtract).then_inc(rt_dve, 1)
            dve.wait_ge(rt_act, 2)
            ch.link(dve.reduce_sum(rs, prob, axis=AX))
            ch.link(dve.reciprocal(rs, rs))
            ch.link(tt(prob, prob, spread(rs, NE), ALU.mult))
            g4 = rview(64, 32).rearrange("p (g q) -> p g q", q=EPG)
            ch.step(tt(pair1[:, :, 0:2], g4[:, :, 0:2], g4[:, :, 2:4], ALU.add))
            ch.step(tt(pair1[:, :, 2:4], g4[:, :, 0:4:2], g4[:, :, 1:4:2], ALU.add))
            ch.step(tt(pair1[:, :, 4:5], g4[:, :, 0:1], g4[:, :, 3:4], ALU.add))
            ch.link(tt(pair1[:, :, 5:6], g4[:, :, 1:2], g4[:, :, 2:3], ALU.add))
            ch.link(dve.reduce_max(gsc, pair1, axis=AX))
            grp = lambda t: t.rearrange("p (m g) -> p m g", m=NT)
            ch.link(dve.reduce_max(gm, grp(gsc), axis=AX))
            ch.link(tt(grp(gtmp), grp(gsc), spread(gm, NGRP), ALU.is_equal))
            ch.link(tt(grp(gtmp), grp(gtmp), rank4.rearrange("p (o g) -> p o g", o=1).to_broadcast([P, NT, NGRP]), ALU.mult))
            ch.link(dve.reduce_max(gm, grp(gtmp), axis=AX))
            ch.link(tt(grp(msk4), grp(gtmp), spread(gm, NGRP), ALU.is_equal))
            mk = rview(192, 32).rearrange("p (g q) -> p g q", q=EPG)
            ch.link(tt(mk, g4, spread(msk4, EPG), ALU.mult))
            ch.link(ts(msk4, msk4, -1.0, None, ALU.add))
            ch.link(tt(mk, mk, spread(msk4, EPG), ALU.add))
            r16 = rank16.rearrange("p (o e) -> p o e", o=1).to_broadcast([P, NT, NE])
            for best, value in ((top1, v1), (top2, v2)):
                ch.link(dve.reduce_max(value, masked, axis=AX))
                ch.link(tt(t16, masked, spread(value, NE), ALU.is_equal))
                ch.link(tt(t16, t16, r16, ALU.mult))
                ch.link(dve.reduce_max(gm, t16, axis=AX))
                ch.link(tt(best, t16, spread(gm, NE), ALU.is_equal))
                ch.link(stt(masked, best, -3.0, masked, ALU.mult, ALU.add))
            tt(chosen, top1, top2, ALU.add).then_inc(chosen_ready, 1)
            ch.link(tt(rs, v1, v2, ALU.add))
            ch.link(dve.reciprocal(rs, rs))
            ch.step(tt(v1, v1, rs, ALU.mult))
            ch.link(tt(v2, v2, rs, ALU.mult))
            ch.step(tt(top1, top1, spread(v1, NE), ALU.mult))
            ch.link(tt(top2, top2, spread(v2, NE), ALU.mult))
            ch.link(tt(gate[:, :, 0:NE], top1, top2, ALU.add))
            dve.wait_ge(chosen_ready, 1)
            ch.link(ts(t16, chosen, -1.0, None, ALU.add))
            dve.wait_ge(rt_pe, 3)
            ch.step(dve.reduce_max(stat[:, 5:6], bank[2][:, 2 * NE:3 * NE], axis=AX))
            ch.link(tt(masked, bank[2][:, 0:2 * NE].rearrange("p (m e) -> p m e", m=NT), chosen, ALU.mult))
            ch.link(tt(pos[:, :, 0:NE], masked, t16, ALU.add))
            dve.tensor_copy(count_i[0:1, 0:1], stat[0:1, 5:6]).then_inc(routed, 1)

            def select(e):
                for m in range(NT):
                    for a in range(2):
                        at = slice(a * CAP, (a + 1) * CAP)
                        p1, g1 = pos[:, m, bass.ds(e + a, 1)], gate[:, m, bass.ds(e + a, 1)]
                        ts(sel[:, m, at], slot_id[:, 0:CAP], p1, None, ALU.is_equal)
                        ins = ts(selg[:, m, at], slot_id[:, 0:CAP], p1, g1, ALU.is_equal, ALU.mult)
                ins.then_inc(sel_ready, 1)

            def experts(n, e, ch):
                for j in (1, 3):
                    dve.wait_ge(m_full[1], 3 * n + j // 2 + 1)
                    for kk in range(4):
                        k = 4 * j + kk
                        ins = ts(xe[:, k, :], hx[1][:, kk * P:(kk + 1) * P], a_mul[:, KT + k:KT + k + 1],
                                 mod[:, 2 * KT + k:2 * KT + k + 1], ALU.mult, ALU.add)
                    ins.then_inc(m_read[1], 1)
                dve.wait_ge(gate_done, n + 1)
                ts(hid, acc[:, :], -CLAMP, None, ALU.max).then_inc(gate_clamped, 1)
                dve.wait_ge(gate_exp, n + 1)
                ch.link(ts(hid, hid, 1.0, None, ALU.add))
                ch.link(dve.reciprocal(hid, hid))
                ch.link(tt(hid, acc[:, :], hid, ALU.mult))
                dve.wait_ge(up_done, n + 1)
                tt(hid, aux[:, :], hid, ALU.mult).then_inc(hid_ready, 1)
                dve.wait_ge(m_full[0], 3 * n + 3)
                select(e + 2)
                for dc in range(2, NP_D):
                    dve.wait_ge(y_done, 4 * n + dc + 1)
                    dve.tensor_copy(ys[:, dc * PANEL:(dc + 1) * PANEL], pw[dc][:, :]).then_inc(y_dve, 1)
                for q in range(NT * NP_D):
                    m, dc = q // NP_D, q % NP_D
                    at = slice(dc * PANEL, (dc + 1) * PANEL)
                    dve.wait_ge(sc_done, 8 * n + q + 1)
                    ch.wait()
                    tt(ytmp, pw[dc][:, :], gates_bc[:, D + dc * PANEL:D + (dc + 1) * PANEL], ALU.mult).then_inc(sc_read, 1)
                    dve.wait_ge(sc_read, GIVEN + 8 * n + q + 1)
                    ch.step(tt(res[:, m, at], res[:, m, at], ytmp, ALU.add))

            ch.wait()
            select(0)
            with dve.Fori(0, NPAIR) as i:
                ch.enter(i, PER_EXPERTS)
                experts(i, 2 * i, ch)
                ch.leave(NPAIR)
            dve.wait_ge(routed, 1)
            most = dve.value_load(count_i[0:1, 0:1], min_val=0, max_val=SEQ)
            ch.wait()
            with dve.If(most > CAP):
                with dve.Fori(1, ROUNDS) as r:
                    rounds = Chain(dve, c_rounds)
                    rounds.turns = (r - 1) * (1 + NPAIR * PER_EXPERTS)
                    rounds.link(ts(pos[:, :, :], pos[:, :, :], -float(CAP), None, ALU.add))
                    select(0)
                    with dve.Fori(0, NPAIR) as i:
                        rounds.enter(i, PER_EXPERTS)
                        experts(r * NPAIR + i, 2 * i, rounds)
                        rounds.leave(NPAIR)
                    rounds.wait()
            dve.nop().then_inc(moe_out, 1)
            dve.wait_ge(sumsq, 2 * NT + NT * NP_D)
            ts(stat[:, 2:4], stat[:, 0:2], 1.0 / D, EPS, ALU.mult, ALU.add).then_inc(var_ready, 1)
            dve.wait_ge(rstd_ready, 3)
            dve.wait_ge(fn_loaded, 16)
            for m in range(NT):
                stt(res[:, m, :], res[:, m, :], stat[:, 2 + m:3 + m], fnorm, ALU.mult, ALU.mult).then_inc(out_ready, 1)


_INS = ["x", "c", "w_in", "w_out", "attn_norm", "ffn_norm", "w_ada", "b_ada", "lambda_q1", "lambda_k1", "lambda_q2",
        "lambda_k2", "diff_subln", "hgrn_lb", "hgrn_norm", "rel_bias", "w_router", "b_router", "w_gate", "w_up",
        "w_down", "final_norm"]


def kernel(**inputs):
    import numpy as _np
    import concourse.bacc as _bacc
    from concourse import mybir as _mybir
    from concourse.bass_utils import run_bass_kernel_spmd as _run

    nc = _bacc.Bacc("TRN2", target_bir_lowering=False, num_devices=1)
    arrays, args = {}, {}
    consts = dict(zip(("consts", "masks", "onehot"), shape_constants()))
    for name, a in [(n, _np.ascontiguousarray(inputs[n])) for n in _INS] + list(consts.items()):
        arrays[f"in_{name}"] = a
        args[name] = nc.dram_tensor(f"in_{name}", a.shape, _mybir.dt.from_np(a.dtype), kind="ExternalInput").ap()
    for name in ("x", "w_in", "w_out", "w_ada", "w_gate", "w_up", "w_down"):
        args[name] = args[name][0]
    out = nc.dram_tensor("out_y", (1, SEQ, D), F32, kind="ExternalOutput").ap()
    build_program(nc, out=out[0], **args)
    r = _run(nc, [arrays], core_ids=[0])
    return r.results[0]["out_y"]
```

```python
import math
from contextlib import ExitStack

import numpy as np

import concourse.bass as bass
from concourse import mybir

F32 = mybir.dt.float32
F32R = mybir.dt.float32r
I32 = mybir.dt.int32
U8 = mybir.dt.uint8
ALU = mybir.AluOpType
ACT = mybir.ActivationFunctionType
AX = mybir.AxisListType.X

P = 128
D = 2048
SEQ = 256
NT = SEQ // P
KT = D // P
PANEL = 512
NP_D = D // PANEL
HD = 128
D_DIFF = D // 2
D_HGRN = D - D_DIFF
NH = D_DIFF // HD
GH = PANEL // HD
NG = NH // GH
QK = HD // 2
CHUNK = 64
BUCKETS = 32
MAX_DISTANCE = 128
NE = 16
NGRP = 4
EPG = NE // NGRP
DE = D // 4
FT = DE // P
CAP = P // 2
NPAIR = NE // 2
ROUNDS = SEQ // CAP
EPS = 1e-6
LAMBDA_INIT = 0.8 - 0.6 * math.exp(-0.3 * 0)
CLAMP = 87.0
SPLIT = 2.0 ** -63
TINY = float(np.finfo(np.float32).tiny)
BIAS_W = 3 * P

COL_QD, COL_KD, COL_VD = 0, D_DIFF, 2 * D_DIFF
COL_QH = 3 * D_DIFF
COL_FH, COL_IH, COL_GH = COL_QH + D_HGRN, COL_QH + 2 * D_HGRN, COL_QH + 3 * D_HGRN

LEVELS = [0, 32, 16, 8, 4, 2, 1, 64]

PER_HGRN, PER_DIFF, PER_EXPERTS = 27 + 4 * 14, 24 + 3 * 14, 3

ROW_C, ROW_AN, ROW_FN, ROW_LB, ROW_SUB, ROW_HN, N_ROWS = 0, 16, 32, 48, 56, 57, 58


def shape_constants():
    n = np.arange(P)
    ident = np.eye(P, dtype=np.float32)
    before = (n[:, None] < n[None, :]).astype(np.float32)
    slot = np.broadcast_to(np.tile(np.arange(CAP), 2)[None, :], (P, P)).astype(np.float32)
    rank = np.broadcast_to(np.concatenate([NE - np.arange(NE), NGRP - np.arange(NGRP)])[None, :], (P, NE + NGRP))
    consts = np.concatenate([ident, before, slot, rank.astype(np.float32)], axis=1)
    masks = []
    for half in LEVELS:
        if half == 0:
            m = n[:, None] == n[None, :]
        else:
            m = (n[:, None] // (2 * half) == n[None, :] // (2 * half)) & (n[:, None] // half % 2 == 0) & (n[None, :] // half % 2 == 1)
        masks.append(m.astype(np.float32))
    masks = np.ascontiguousarray(np.stack(masks, axis=1).reshape(P, len(LEVELS) * P))
    rel = 2 * P - 1 - np.arange(BIAS_W)
    exact = BUCKETS // 2
    far = np.maximum(rel, 1).astype(np.float32)
    large = exact + (np.log(far / np.float32(exact)) / np.float32(math.log(MAX_DISTANCE / exact)) * (BUCKETS - exact)).astype(np.int32)
    bucket = np.where(rel < exact, np.maximum(rel, 0), np.minimum(large, BUCKETS - 1))
    onehot = np.zeros((BUCKETS + 1, BIAS_W), np.float32)
    onehot[bucket, np.arange(BIAS_W)] = 1.0
    onehot[:, rel < 0] = 0.0
    onehot[BUCKETS, rel < 0] = -1e30
    return consts, masks, onehot


class Chain:

    def __init__(self, eng, sem):
        self.eng, self.sem, self.n, self.turns = eng, sem, 0, 0

    def step(self, ins):
        ins.then_inc(self.sem, 1)
        self.n += 1

    def wait(self):
        self.eng.wait_ge(self.sem, self.turns + self.n)

    def link(self, ins):
        self.step(ins)
        self.wait()

    def enter(self, i, per):
        self.before, self.per, self.outer = self.n, per, self.turns
        self.turns = self.turns + i * per

    def leave(self, times):
        assert self.n - self.before == self.per, (self.sem, self.n - self.before)
        self.n += self.per * (times - 1)
        self.turns = self.outer


def build_program(nc, x, c, w_in, w_out, attn_norm, ffn_norm, w_ada, b_ada, lambda_q1, lambda_k1, lambda_q2,
                  lambda_k2, diff_subln, hgrn_lb, hgrn_norm, rel_bias, w_router, b_router, w_gate, w_up, w_down,
                  final_norm, consts, masks, onehot, out):
    with ExitStack() as ctx:
        def sb(name, shape, dt=F32):
            return ctx.enter_context(nc.sbuf_tensor(name, shape, dt))

        def sem(name):
            return ctx.enter_context(nc.semaphore(name))

        SLOT = 8 * PANEL
        res = sb("res", [P, NT, D])
        mixT = sb("mixT", [P, KT, SEQ])
        gates_bc = sb("gates_bc", [P, 2 * D])
        cst = sb("cst", [P, 3 * P + NE + NGRP])
        msk = sb("msk", [P, len(LEVELS), P], U8)
        ones = sb("ones", [P, P])
        mean_w = sb("mean_w", [P, P])
        ccol = sb("ccol", [P, KT])
        cact = sb("cact", [P, KT, 32])
        resets = sb("resets", [P, SEQ])
        rows = sb("rows", [N_ROWS, P])
        brows = sb("brows", [64, P])
        cols = sb("cols", [P, N_ROWS])
        bcols = sb("bcols", [P, 64])
        mod = sb("mod", [P, 64])
        a_mul = sb("a_mul", [P, 2 * KT])
        lb = sb("lb", [P, 5, NH])
        lam = sb("lam", [1, 4, QK])
        lams = sb("lams", [1, 8])
        stat = sb("stat", [P, 64])
        count_i = sb("count_i", [1, 2], I32)
        relb = sb("relb", [BUCKETS + 1, 2 * NH])
        nhalf = sb("nhalf", [P, 1])
        hstat = sb("hstat", [P, 2, 8])
        waiter = sb("waiter", [1, 2 * len(LEVELS)])
        pos = sb("pos", [P, NT, NE + 2])
        gate = sb("gate", [P, NT, NE + 2])
        arow0 = sb("arow0", [P, PANEL])
        with ExitStack() as shared:
            ring = shared.enter_context(nc.sbuf_tensor("ring", [P, 6, SLOT], F32))
            hT = shared.enter_context(nc.sbuf_tensor("hT", [P, KT, SEQ], F32))
            work = shared.enter_context(nc.sbuf_tensor("work", [P, 7168], F32))
        sb("ring_slots_0_to_3", [P, 4, SLOT])
        w_part0 = sb("w_parts_even", [P, 2, 4, PANEL], F32R)
        mix_hgrn = sb("mix_parts_hgrn", [P, 2, KT // 2, SEQ], F32R)
        mix_diff = sb("mix_parts_attention", [P, 2, KT // 2, SEQ], F32R)
        w_part1 = sb("w_parts_odd", [P, 2, 4, PANEL], F32R)
        w_part = [w_part0, w_part1]

        ident = cst[:, 0:P]
        before = cst[:, P:2 * P]
        slot_id = cst[:, 2 * P:3 * P]
        rank16 = cst[:, 3 * P:3 * P + NE]
        rank4 = cst[:, 3 * P + NE:3 * P + NE + NGRP]

        head = ring[:, 4:6, :].rearrange("p a (b n) -> p (a b) n", n=GH * SEQ)

        def hbuf(n):
            return head[:, n, :]

        qd, kd, vd, qh, kh, bh, gh, vh = (hbuf(n) for n in range(8))
        heads = lambda t: t.rearrange("p (h t) -> p h t", h=GH)
        toks = lambda t: t.rearrange("p (m n) -> p m n", m=NT)
        slotv = lambda s: ring[:, s, :] if s < 6 else mixT[:, :, :].rearrange("p k t -> p (k t)")
        panelv = lambda s: ring[:, s, :].rearrange("p (k n) -> p k n", n=PANEL)
        dbuf = [work[:, 0:1024], work[:, 1024:2048]]
        zbuf = [work[:, 2048:3072], work[:, 3072:4096]]
        sc_diag = work[:, 4096:5120]
        sc_off = work[:, 5120:5632]
        ohb = work[:, 5632:6656]
        sbuf = work[:, 0:1536].rearrange("p (b s n) -> p b s n", b=2, s=2)
        bias = work[:, 1536:3072].rearrange("p (b s n) -> p b s n", b=2, s=2)
        aT = work[:, 3072:4608].rearrange("p (h n) -> p h n", h=GH)
        odb = work[:, 4608:5632]
        amix = work[:, 5632:6016]
        osq_d = work[:, 0:1024]
        rs_d = work[:, 5632:6656]
        tmp = work[:, 4608:5120]
        squares = [work[:, 4096:4608], work[:, 5632:6144], work[:, 6144:6656]]
        arow = [arow0[:, :], work[:, 6656:7168]]
        xn = mixT[:, :, :].rearrange("p k t -> p (k t)").rearrange("p (m n) -> p m n", m=NT)
        xn2 = hT[:, :, :].rearrange("p k t -> p (k t)").rearrange("p (m n) -> p m n", m=NT)
        h2T = mixT
        xe = work[:, 0:2048].rearrange("p (k s) -> p k s", k=KT)
        ys = work[:, 2048:4096]
        sel = work[:, 4096:4352].rearrange("p (m s) -> p m s", m=NT)
        selg = work[:, 4352:4608].rearrange("p (m s) -> p m s", m=NT)
        selT = work[:, 4608:4864]
        hid = work[:, 4864:5376]
        hidT = work[:, 5376:5888].rearrange("p (f s) -> p f s", f=FT)
        fnorm = gates_bc[:, 0:D]
        wr = work[:, 5120:5120 + KT * 32].rearrange("p (k e) -> p k e", k=KT)
        lt = work[:, KT * 32:KT * 32 + SEQ]
        rt = work[:, 1024:1536]

        def rview(n, w):
            return rt[:, n:n + w]

        logit = rview(0, 32).rearrange("p (m e) -> p m e", m=NT)
        prob = rview(64, 32).rearrange("p (m e) -> p m e", m=NT)
        pair1 = rview(96, 48).rearrange("p (g q) -> p g q", q=6)
        gsc = rview(144, 8)
        gtmp = rview(152, 8)
        msk4 = rview(160, 8)
        masked = rview(192, 32).rearrange("p (m e) -> p m e", m=NT)
        top1 = rview(224, 32).rearrange("p (m e) -> p m e", m=NT)
        top2 = rview(256, 32).rearrange("p (m e) -> p m e", m=NT)
        t16 = rview(288, 32).rearrange("p (m e) -> p m e", m=NT)
        chosen = rview(320, 32).rearrange("p (m e) -> p m e", m=NT)


        bias_rows = nc.dram_tensor("bias_rows", (2 * NH, BIAS_W), F32, kind="Internal")

        bank = [ctx.enter_context(nc.psum_tensor(f"bank{b}", [P, PANEL], F32)) for b in range(8)]
        pw = bank[0:4]
        acc, aux = bank[4], bank[5]
        hx = bank[6:8]

        mix_high, mix_low = sem("mix_high_parts"), sem("mix_low_parts")
        w_high, w_low, w_used = sem("w_out_high_parts"), sem("w_out_low_parts"), sem("w_out_parts_used")
        s_x = sem("x_loaded")
        s_small = sem("vectors_loaded")
        s_bload = sem("gate_bias_loaded")
        s_const, mask_ready = sem("constants_set"), sem("masks_ready")
        full = [sem(f"slot{s}_full") for s in range(4)]
        ada_full = [sem(f"slot{s}_full_of_ada") for s in range(2)]
        free = {s: sem(f"slot{s}_free") for s in (0, 2)}
        efull = [sem(f"expert_slot{s}_full") for s in range(7)]
        efree = [sem(f"expert_slot{s}_free") for s in range(7)]
        wr_zeroed = sem("router_padding_set")
        ada_a, ada_b = sem("ada_panel_a_done"), sem("ada_panel_b_done")
        ada_copied = sem("ada_row_copied")
        aux_full, aux_read = sem("aux_full"), sem("aux_read")
        hx_full = [sem(f"hx{b}_full") for b in range(2)]
        hx_read = [sem(f"hx{b}_read") for b in range(2)]
        pre_t, pre_v, pre_d = sem("small_transposed"), sem("small_copied"), sem("small_prepared")
        cact_ready = sem("cact_ready")
        lam_ready = sem("lambda_ready")
        brow_ready, brow_saved = sem("bias_row_ready"), sem("bias_row_saved")
        sumsq, var_ready, rstd_ready = sem("sumsq_ready"), sem("variance_ready"), sem("rstd_ready")
        xn_ready = sem("xn_ready")
        xt_full = sem("x_transposed")
        xt_a, xt_v = sem("x_transposed_copied_act"), sem("x_transposed_copied_vec")
        mod_ready = sem("first_modulation_ready")
        h_ready, h_ready2 = sem("h_first_half_ready"), sem("h_second_half_ready")
        win_done, win_read = sem("w_in_bank_done"), sem("w_in_bank_copied")
        f_clamped, f_exp = sem("f_clamped"), sem("f_exp")
        f_split, f_log = sem("f_split"), sem("f_logs")
        b_ready = sem("cumulated_decay_ready")
        d_ready, e_ready = sem("decay_exponent_ready"), sem("decay_ready")
        z_ready = sem("decayed_operand_ready")
        g_clamped, g_exp = sem("g_clamped"), sem("g_exp")
        or_log, or_ready = sem("head_log_ready"), sem("head_rstd_ready")
        hgrn_out = sem("hgrn_group_out")
        bias_loaded = [sem(f"bias{b}_loaded") for b in range(2)]
        max_ready, p_ready, a_ready = sem("score_max_ready"), sem("probs_ready"), sem("mixed_probs_ready")
        diff_out = sem("diff_group_out")
        wout_done, wout_read = sem("w_out_bank_done"), sem("w_out_bank_read")
        res_ready = sem("residual_chunk_ready")
        wr_loaded = sem("router_loaded")
        rt_pe, rt_act, rt_dve = sem("router_pe"), sem("router_act"), sem("router_dve")
        chosen_ready = sem("experts_chosen")
        routed = sem("routed")
        m_full = [sem(f"gather{b}_full") for b in range(2)]
        m_read = [sem(f"gather{b}_read") for b in range(2)]
        sel_ready = sem("selection_ready")
        gate_done, up_done = sem("gate_done"), sem("up_done")
        gate_clamped, gate_exp = sem("gate_clamped"), sem("gate_exp")
        hid_ready = sem("hidden_ready")
        y_done, y_gated = sem("down_done"), sem("down_gated")
        sc_done, sc_read = sem("scatter_done"), sem("scatter_read")
        fn_loaded = sem("final_norm_loaded")
        moe_out = sem("moe_out")
        out_ready, out_saved = sem("out_ready"), sem("out_saved")
        c_dve, c_pool, c_rounds = sem("vector_steps"), sem("gpsimd_steps"), sem("vector_round_steps")

        block = ctx.enter_context(nc.Block())

        ADA0 = 4
        WIN_G, WIN_A = 3 * GH + NT, 2 * GH + NT
        WIN_ALL = NG * (WIN_G + WIN_A)
        AUX_G = 8
        AUX_A = AUX_G + 6 * NG
        AUX_O = AUX_A + 9 * NG
        HX_G = [11, 10]
        HX_A = 6
        hx_base = [NG * n for n in HX_G]

        def w_rows(w, row, col):
            return w[row:row + 8 * P, bass.ds(col, PANEL)].rearrange("(k p) n -> p k n", p=P)

        GIVEN = 1
        given = [free[0], free[2], ada_a, ada_b, win_done, win_read, ada_copied, aux_read, hgrn_out, diff_out,
                 hid_ready, sc_read] + hx_read + m_read

        def w_slot(n, q):
            return (0 if n == 3 else 2) + q // 2

        def w_filled(n, q):
            return 16 * (ADA0 + 1) if n == 3 else 16 * (ADA0 + 7 * NG + n + 1)

        def w_released(at):
            n, q = (at + 2) // 4, (at + 2) % 4
            return NT * (n + 1) if q == 3 else 3 * n + q - 1

        @block.sync
        def _(sp):
            for signal in given:
                sp.sem_inc(signal, GIVEN)
            for m in range(NT):
                sp.dma_start(res[:, m, :], x[m * P:(m + 1) * P, :]).then_inc(s_x, 16)
            small = lambda dst, src: sp.dma_start(dst, src).then_inc(s_small, 16)
            for n, v in enumerate((lambda_q1, lambda_q2, lambda_k1, lambda_k2)):
                small(lam[0:1, n, :], v)
            small(relb[0:BUCKETS, :], rel_bias)
            small(work[0:BUCKETS + 1, 6656 - BIAS_W:6656], onehot)
            small(work[:, 0:len(LEVELS) * P], masks)
            small(stat[:, 8:8 + NE], b_router.rearrange("(o e) -> o e", o=1).to_broadcast([P, NE]))

            def load(w, s, half, col, row=None):
                sp.dma_start(panelv(s), w_rows(w, (half if row is None else row) * 8 * P, col)).then_inc(full[s], 16)

            with sp.Fori(0, ADA0) as i:
                for pair, done in ((0, ada_a), (1, ada_b)):
                    col = (2 * i + pair) * PANEL
                    sp.wait_ge(free[2 * pair], GIVEN + i)
                    load(w_ada, 2 * pair, 0, col)
                    sp.wait_ge(done, GIVEN + i)
                    load(w_ada, 2 * pair + 1, 1, col)
            with sp.Fori(0, NG) as i:
                for t, (wcol, nbanks) in enumerate(((COL_FH, 0), (COL_QH, GH), (COL_IH, 2 * GH), (COL_GH, 2 * GH + NT))):
                    n = 4 * i + t
                    sp.wait_ge(free[2], GIVEN + ADA0 + n)
                    load(w_in, 2, 0, wcol + i * PANEL)
                    if t == 0:
                        sp.wait_ge(ada_b, GIVEN + ADA0)
                    sp.wait_ge(win_done, GIVEN + WIN_G * i + nbanks)
                    load(w_in, 3, 1, wcol + i * PANEL)
            for n, col in enumerate((2 * D, 5 * D)):
                sp.dma_start(gates_bc[:, n * D:(n + 1) * D], b_ada[0:1, col:col + D].to_broadcast([P, D])).then_inc(s_bload, 16)
            with sp.Fori(0, NG) as j:
                for t, (wcol, nbanks) in enumerate(((COL_QD, 0), (COL_KD, GH), (COL_VD, 2 * GH))):
                    n = ADA0 + 4 * NG + 3 * j + t
                    sp.wait_ge(free[2], GIVEN + n)
                    load(w_in, 2, 0, wcol + j * PANEL)
                    sp.wait_ge(win_done, GIVEN + WIN_G * NG + WIN_A * j + nbanks)
                    load(w_in, 3, 1, wcol + j * PANEL)
            n = ADA0 + 4 * NG + 3 * NG
            sp.wait_ge(free[2], GIVEN + n)
            load(w_out, 2, 1, 0)
            sp.wait_ge(win_done, GIVEN + WIN_ALL)
            load(w_out, 3, 0, 0)
            sp.wait_ge(free[2], GIVEN + n + 1)
            load(w_out, 2, 1, PANEL)
            sp.wait_ge(w_low, 2)
            load(w_out, 3, 0, PANEL)
            sp.wait_ge(w_low, 4)
            load(w_out, 2, 1, 2 * PANEL)
            sp.wait_ge(w_low, 6)
            load(w_out, 3, 0, 2 * PANEL)
            sp.wait_ge(free[0], GIVEN + n + 2)
            load(w_out, 0, 1, 3 * PANEL)
            sp.wait_ge(ada_a, GIVEN + n + 2)
            load(w_out, 1, 0, 3 * PANEL)

            def expert_loads(n, e, first):
                def pick(w, a, rows):
                    return w[bass.ds(e + a, 1), rows, :].rearrange("o p n -> (o p) n")

                kin = lambda w, q, a: pick(w, a, slice(q * 4 * P, (q + 1) * 4 * P)).rearrange("(k p) n -> p k n", p=P)
                dst = lambda s, a: slotv(s).rearrange("p (e k n) -> p e k n", e=2, k=4)[:, a]
                kdn = lambda q, a: pick(w_down, a, slice(q * P, (q + 1) * P))
                dsd = lambda s, a: slotv(s).rearrange("p (e n) -> p e n", e=2)[:, a]
                plan = [(w_gate, 0, 0, efree[0], n), (w_gate, 1, 1, up_done, n), (w_gate, 2, 2, efree[2], 2 * n),
                        (w_gate, 3, 3, efree[3], n), (w_up, 0, 4, efree[4], 2 * n), (w_up, 1, 5, y_done, NP_D * n),
                        (w_up, 2, 6, efree[6], n), (w_up, 3, 1, efree[1], n + 1),
                        (None, 0, 2, efree[2], 2 * n + 1), (None, 1, 3, gate_done, n + 1),
                        (None, 2, 4, efree[4], 2 * n + 1), (None, 3, 5, efree[5], n + 1)]
                before_first = [(w_low, 12), (w_low, 14), (w_low, 8), (w_low, 10), (wout_done, 4 * NT),
                                (wout_done, 4 * NT), (rt_pe, 1)]
                for k, (w, q, s, released, value) in enumerate(plan):
                    if first and k < len(before_first):
                        sp.wait_ge(*before_first[k])
                    else:
                        sp.wait_ge(released, value)
                    for a in range(2):
                        if w is None:
                            sp.dma_start(dsd(s, a), kdn(q, a)).then_inc(efull[s], 16)
                        else:
                            sp.dma_start(dst(s, a), kin(w, q, a)).then_inc(efull[s], 16)

            expert_loads(0, 0, True)
            with sp.Fori(1, NPAIR) as i:
                expert_loads(i, 2 * i, False)
            sp.wait_ge(routed, 1)
            most = sp.value_load(count_i[0:1, 0:1], min_val=0, max_val=SEQ)
            with sp.If(most > CAP):
                with sp.Fori(1, ROUNDS) as r:
                    with sp.Fori(0, NPAIR) as i:
                        expert_loads(r * NPAIR + i, 2 * i, False)
            for m in range(NT):
                for a, at in enumerate((slice(0, D // 2), slice(D // 2, D))):
                    sp.wait_ge(out_ready, 2 * m + a + 1)
                    sp.dma_start(out[m * P:(m + 1) * P, at], res[:, m, at]).then_inc(out_saved, 16)
            sp.wait_ge(out_saved, 16 * 2 * NT)

        @block.gpsimd
        def _(pool):
            ch = Chain(pool, c_pool)
            half = nhalf[:, 0:1]
            ch.link(pool.memset(nhalf[:, :], -0.5))
            pool.wait_ge(var_ready, 1)
            pool.tensor_tensor(stat[:, 2:4], stat[:, 2:4], half.to_broadcast([P, NT]), ALU.pow).then_inc(rstd_ready, 1)
            pool.wait_ge(brow_ready, 1)
            pool.dma_start(bias_rows.ap(), work[0:2 * NH, 6656:6656 + BIAS_W]).then_inc(brow_saved, 16)

            def load_ada_half(n, col, s, used):
                pool.wait_ge(used, GIVEN + n)
                pool.dma_start(panelv(s), w_rows(w_ada, s * 8 * P, col)).then_inc(ada_full[s], 16)

            def load_ada(n, col):
                load_ada_half(n, col, 0, free[0])
                load_ada_half(n, col, 1, ada_a)

            pool.wait_ge(full[2], 16 * (ADA0 + 1))
            with pool.Fori(0, NG) as i:
                ch.enter(i, 1)
                for t in range(3):
                    load_ada(ADA0 + 4 * i + t, 3 * D + (4 * i + t) * PANEL)
                pool.wait_ge(b_ready, i + 1)
                for lv, n in enumerate(LEVELS[1:] + [P]):
                    dt = dbuf[lv % 2]
                    if lv >= 2:
                        pool.wait_ge(z_ready, 8 * i + lv - 1)
                    if n < P:
                        b4 = bh.rearrange("p (q s n) -> p q s n", s=2, n=n)
                        d4 = dt.rearrange("p (q s n) -> p q s n", s=2, n=n)
                        ref = b4[:, :, 0, n - 1:n].to_broadcast([P, GH * SEQ // (2 * n), n])
                        if n < CHUNK:
                            pool.tensor_tensor(d4[:, :, 0, :], ref, b4[:, :, 0, :], ALU.subtract)
                            pool.tensor_tensor(d4[:, :, 1, :], b4[:, :, 1, :], ref, ALU.subtract).then_inc(d_ready, 1)
                        else:
                            pool.tensor_tensor(d4[:, :, 0, :], ref, b4[:, :, 0, :], ALU.subtract).then_inc(d_ready, 1)
                    else:
                        b4 = bh.rearrange("p (h c n) -> p h c n", c=4, n=CHUNK)
                        d4 = dt.rearrange("p (h c n) -> p h c n", c=4, n=CHUNK)
                        end = [b4[:, :, q, CHUNK - 1:CHUNK].to_broadcast([P, GH, CHUNK]) for q in range(3)]
                        ch.step(pool.tensor_tensor(d4[:, :, 0, :], end[0], b4[:, :, 0, :], ALU.subtract))
                        pool.tensor_tensor(d4[:, :, 1, :], end[1], b4[:, :, 1, :], ALU.subtract)
                        pool.tensor_tensor(d4[:, :, 3, :], b4[:, :, 3, :], end[2], ALU.add)
                        ch.wait()
                        pool.tensor_tensor(d4[:, :, 0, :], d4[:, :, 0, :], end[1], ALU.add).then_inc(d_ready, 1)
                load_ada(ADA0 + 4 * i + 3, 3 * D + (4 * i + 3) * PANEL)
                ch.leave(NG)

            def load_bias(h, b):
                for col, n, at in ((0, 2 * P, 0), (P, P, 2 * P)):
                    shifted = bass.AP(tensor=bias_rows, offset=2 * h * BIAS_W + col, ap=[[1, P], [BIAS_W, 2], [1, n]])
                    pool.dma_start(bias[:, b, :, at:at + n], shifted).then_inc(bias_loaded[b], 16)

            pool.wait_ge(brow_saved, 16)
            with pool.Fori(0, NG) as j:
                for h in range(GH):
                    if h < 3:
                        load_ada(ADA0 + 4 * NG + 3 * j + h, (8 + 3 * j) * PANEL if h == 0 else (8 + h + 11 * j) * PANEL)
                    if h == 0:
                        pool.wait_ge(hgrn_out, GIVEN + NG)
                    pool.wait_ge(hx_read[1], GIVEN + hx_base[1] + HX_A * j + (h - 3 if h < 2 else h - 1))
                    load_bias(GH * j + h, h % 2)

            n = ADA0 + 7 * NG
            load_ada(n, 22 * PANEL)
            pool.wait_ge(aux_full, AUX_O - 6)
            for kk in range(KT):
                if kk % 8 == 0:
                    pool.wait_ge(ada_full[kk // 8], 16 * (n - ADA0 + 1))
                panel = panelv(kk // 8)[:, kk % 8, :]
                if kk == 0:
                    ins = pool.tensor_scalar(arow[0], panel, ccol[:, kk:kk + 1], None, ALU.mult)
                else:
                    ch.step(pool.tensor_scalar(panel, panel, ccol[:, kk:kk + 1], None, ALU.mult))
                    ch.wait()
                    ins = pool.tensor_tensor(arow[0], panel, arow[0], ALU.add)
                if kk == KT // 2 - 1:
                    ins.then_inc(free[0], 1)
                    load_ada_half(n + 1, 23 * PANEL, 0, free[0])
                elif kk == KT - 1:
                    ins.then_inc(ada_a, 1)
                    load_ada_half(n + 1, 23 * PANEL, 1, ada_a)
                else:
                    ch.step(ins)
                    ch.wait()
            for k in range(2, 4):
                pool.wait_ge(var_ready, k)
                pool.tensor_tensor(stat[:, 2:4], stat[:, 2:4], half.to_broadcast([P, NT]), ALU.pow).then_inc(rstd_ready, 1)

        @block.tensor
        def _(pe):
            def mm(o, lhsT, rhs, start=True, stop=True):
                return pe.matmul(o, lhsT, rhs, start=start, stop=stop)

            pe.wait_ge(s_small, 16 * 17)
            pe.wait_ge(s_const, 1)
            pe.transpose(aux[:, 0:N_ROWS], rows[:, :], ident[0:N_ROWS, 0:N_ROWS]).then_inc(pre_t, 1)
            pe.transpose(acc[:, 0:64], brows[:, :], ident[0:64, 0:64]).then_inc(pre_t, 1)
            mm(hx[1][0:2 * NH, 0:BIAS_W], relb[:, :], work[0:BUCKETS + 1, 6656 - BIAS_W:6656]).then_inc(pre_t, 1)
            pe.wait_ge(lam_ready, 1)
            mm(hx[0][:, 0:1], ones[0:1, :], lams[0:1, 4:5]).then_inc(pre_t, 1)
            pe.wait_ge(xn_ready, NT)
            for q in range(KT // 2):
                if q >= 4:
                    pe.wait_ge((xt_a, xt_v)[q % 2], (q - 4) // 2 + 1)
                for k in range(2):
                    for m in range(NT):
                        ins = pe.transpose(pw[q % 4][:, k * SEQ + m * P:k * SEQ + (m + 1) * P],
                                           xn[:, m, (2 * q + k) * P:(2 * q + k + 1) * P], ident)
                ins.then_inc(xt_full, 1)
            pe.wait_ge(cact_ready, 1)
            pe.wait_ge(pre_v, 6)
            pe.wait_ge(brow_ready, 1)

            def ada(n, s, filled, done):
                pe.wait_ge(ada_copied, GIVEN + n)
                for half in range(2):
                    pe.wait_ge(full[s + half], filled)
                    for k in range(8):
                        q = k % 4
                        ins = mm(acc[32 * q:32 * q + 32, :], cact[:, 8 * half + k, :], panelv(s + half)[:, k, :],
                                 start=half == 0 and k < 4, stop=half == 1 and k >= 4)
                    ins.then_inc(done if half else free[s], 1)

            def ada_columns(row, use):
                pe.wait_ge(aux_read, GIVEN + use)
                for q in range(4):
                    ins = pe.transpose(aux[:, q * P:(q + 1) * P], arow[row][:, q * P:(q + 1) * P], ident)
                ins.then_inc(aux_full, 1)

            def ada_spread(row, use):
                pe.wait_ge(aux_read, GIVEN + use)
                mm(aux[:, :], ones[:, :], arow[row]).then_inc(aux_full, 1)

            def project_T(filled, banks, hooks, first=False):
                for half in range(2):
                    pe.wait_ge(full[2 + half], filled)
                    wp = panelv(2 + half)
                    order = [(k, b) for k in range(8) for b in range(GH)] if half == 0 else \
                            [(k, b) for b in range(GH) for k in range(8)]
                    if half and first:
                        pe.wait_ge(h_ready2, 1)
                    for at, (k, b) in enumerate(order):
                        if half == 0 and first and at % 16 == 0:
                            pe.wait_ge(h_ready, at // 16 + 1)
                        if half == 0 and k == 0:
                            pe.wait_ge(win_read, GIVEN + banks[b])
                        ins = mm(pw[b][:, 0:SEQ], wp[:, k, b * P:(b + 1) * P], hT[:, 8 * half + k, :],
                                 start=half == 0 and k == 0, stop=half == 1 and k == 7)
                        if half and k == 7:
                            ins.then_inc(win_done, 1)
                        elif half == 0 and at == len(order) - 1:
                            ins.then_inc(free[2], 1)
                        if at % 8 == 7 and hooks:
                            hooks.pop(0)()
                for hook in hooks:
                    hook()

            def project(filled, banks, hooks):
                for half in range(2):
                    pe.wait_ge(full[2 + half], filled)
                    wp = panelv(2 + half)
                    order = [(k, m) for k in range(8) for m in range(NT)] if half == 0 else \
                            [(k, m) for m in range(NT) for k in range(8)]
                    for at, (k, m) in enumerate(order):
                        if half == 0 and k == 0:
                            pe.wait_ge(win_read, GIVEN + banks[m])
                        ins = mm(pw[m][:, :], hT[:, 8 * half + k, m * P:(m + 1) * P], wp[:, k, :],
                                 start=half == 0 and k == 0, stop=half == 1 and k == 7)
                        if half and k == 7:
                            ins.then_inc(win_done, 1)
                        elif half == 0 and at == len(order) - 1:
                            ins.then_inc(free[2], 1)
                        if at % 4 == 3 and hooks:
                            hooks.pop(0)()
                for hook in hooks:
                    hook()

            def norm_sums(outs, use, square):
                for q in range(2):
                    for b in range(2):
                        pe.wait_ge(hx_read[b], GIVEN + outs[b] + q + 1)
                    pe.wait_ge(aux_read, GIVEN + use + q)
                    for h in range(2):
                        ins = mm(aux[:, h * SEQ:(h + 1) * SEQ], mean_w[:, :], square[:, (2 * q + h) * SEQ:(2 * q + h + 1) * SEQ])
                    ins.then_inc(aux_full, 1)

            with pe.Fori(0, ADA0) as i:
                for t, (s, done) in enumerate(((0, ada_a), (2, ada_b))):
                    ada(2 * i + t, s, 16 * i + 16, done)
                    pe.wait_ge(ada_copied, GIVEN + 2 * i + t + 1)
                    ada_columns(0, 2 * i + t)

            def level(i, lv):
                z = zbuf[(lv - 1) % 2]
                if lv == 0:
                    pe.wait_ge(win_read, GIVEN + WIN_G * i + 2 * GH)
                else:
                    pe.wait_ge(z_ready, 8 * i + lv)
                for b in range(2):
                    pe.wait_ge(hx_read[b], GIVEN + HX_G[b] * i + lv)
                    for h in range(2):
                        for m in range(NT):
                            at = (2 * b + h) * SEQ + m * P
                            o = hx[b][:, h * SEQ + m * P:h * SEQ + (m + 1) * P]
                            ins = mm(o, (kh if lv == 0 else z)[:, at:at + P], (qh if lv == 0 else z)[:, at:at + P])
                    ins.then_inc(hx_full[b], 1)

            def level_across(i):
                z = zbuf[1]
                pe.wait_ge(z_ready, 8 * i + 8)
                pe.wait_ge(hx_read[0], GIVEN + HX_G[0] * i + 8)
                for h in range(GH):
                    ins = mm(hx[0][:, h * P:(h + 1) * P], z[:, h * SEQ:h * SEQ + P], z[:, h * SEQ + P:(h + 1) * SEQ])
                ins.then_inc(hx_full[0], 1)

            nop = lambda: None
            with pe.Fori(0, NG) as i:
                w0 = WIN_G * i
                panels = [[w0] * 4, [w0 + b + 1 for b in range(4)], [w0 + GH + b + 1 for b in range(NT)],
                          [w0 + 2 * GH + b + 1 for b in range(NT)] + [w0 + GH + b + 1 for b in range(NT, 4)]]
                u0 = AUX_G + 6 * i

                def turn_ada(t, use):
                    pe.wait_ge(ada_a, GIVEN + ADA0 + 4 * i + t + 1)
                    ada_columns(t % 2, use)

                def outputs(h):
                    b = h % 2
                    if h == 0:
                        pe.wait_ge(win_read, GIVEN + w0 + 2 * GH + NT)
                    pe.wait_ge(hx_read[b], GIVEN + HX_G[b] * i + 9 - b + h // 2)
                    o = hx[b]
                    vv = toks(vh)[:, :, h * HD:(h + 1) * HD]
                    mm(o[:, 0:P], vv[:, 0, :], sc_diag[:, h * SEQ:h * SEQ + P])
                    mm(o[:, P:SEQ], vv[:, 0, :], sc_off[:, h * P:(h + 1) * P], stop=False)
                    mm(o[:, P:SEQ], vv[:, 1, :], sc_diag[:, h * SEQ + P:(h + 1) * SEQ], start=False).then_inc(hx_full[b], 1)

                levels = [lambda lv=lv: level(i, lv) for lv in range(8)]
                beside = [[], [nop, lambda: turn_ada(0, u0)],
                          [nop, nop, nop, lambda: turn_ada(1, u0 + 1)] + levels[0:4],
                          levels[4:8] + [lambda: (level_across(i), turn_ada(2, u0 + 2)),
                                         lambda: (outputs(0), outputs(1)), lambda: (outputs(2), outputs(3))]]
                for t in range(4):
                    filled = 16 * (ADA0 + 4 * i + t + 1)
                    if t == 2:
                        project(filled, panels[t], beside[t])
                    else:
                        project_T(filled, panels[t], beside[t], t == 0)
                norm_sums([HX_G[b] * i + 9 - b for b in range(2)], u0 + 3, zbuf[0])
                turn_ada(3, u0 + 5)

            def scores(j, h):
                for s in range(2):
                    pe.wait_ge(hx_read[s], GIVEN + hx_base[s] + HX_A * j + h)
                for s in range(2):
                    r = slice(s * QK, (s + 1) * QK)
                    q, k = heads(qd)[r, h, :], heads(kd)[r, h, :]
                    mm(hx[s][:, 0:SEQ], q[:, P:SEQ], k)
                    mm(hx[s][:, SEQ:SEQ + P], q[:, 0:P], k[:, 0:P]).then_inc(hx_full[s], 1)

            def probs_T(j, h, use):
                pe.wait_ge(a_ready, GH * j + h + 1)
                pe.wait_ge(aux_read, GIVEN + use)
                for at, col in ((0, 2 * P), (P, 0), (2 * P, P)):
                    ins = pe.transpose(aux[:, at:at + P], amix[:, col:col + P], ident)
                ins.then_inc(aux_full, 1)

            with pe.Fori(0, NG) as j:
                w0 = WIN_G * NG + WIN_A * j
                a0 = AUX_A + 9 * j
                panels = [[w0] * 4, [w0 + b + 1 for b in range(4)], [w0 + GH + b + 1 for b in range(NT)]]

                def turn_ada(t, use):
                    pe.wait_ge(ada_a, GIVEN + ADA0 + 4 * NG + 3 * j + t + 1)
                    ada_spread(t % 2, use)

                for t in range(3):
                    filled = 16 * (ADA0 + 4 * NG + 3 * j + t + 1)
                    if t == 0:
                        project_T(filled, panels[t], [])
                    elif t == 1:
                        project_T(filled, panels[t], [nop, lambda: turn_ada(0, a0), nop, nop, nop, lambda: turn_ada(1, a0 + 1)])
                    else:
                        pe.wait_ge(win_read, GIVEN + w0 + 2 * GH)
                        scores(j, 0)
                        project(filled, panels[t], [
                            lambda: (turn_ada(2, a0 + 2), scores(j, 1)), lambda: scores(j, 2),
                            lambda: (probs_T(j, 0, a0 + 3), scores(j, 3)), lambda: probs_T(j, 1, a0 + 4),
                            lambda: probs_T(j, 2, a0 + 5), lambda: probs_T(j, 3, a0 + 6)])
                pe.wait_ge(win_read, GIVEN + w0 + WIN_A)
                for h in range(GH):
                    b = h % 2
                    pe.wait_ge(aux_read, GIVEN + a0 + 4 + h)
                    pe.wait_ge(hx_read[b], GIVEN + hx_base[b] + HX_A * j + 4 + h // 2)
                    vv = toks(vd)[:, :, h * HD:(h + 1) * HD]
                    o = hx[b]
                    mm(o[:, 0:P], vv[:, 0, :], aT[:, h, 0:P])
                    mm(o[:, P:SEQ], vv[:, 0, :], aT[:, h, P:2 * P], stop=False)
                    mm(o[:, P:SEQ], vv[:, 1, :], aT[:, h, 2 * P:3 * P], start=False).then_inc(hx_full[b], 1)
                norm_sums([hx_base[b] + HX_A * j + 4 for b in range(2)], a0 + 7, osq_d)

            def out_first_half():
                pe.wait_ge(win_read, GIVEN + WIN_ALL)
                pe.wait_ge(full[2], 16 * (used + 1))
                pe.wait_ge(hgrn_out, GIVEN + NG)
                for k in range(8):
                    for m in range(NT):
                        ins = mm(pw[m][:, :], mixT[:, 8 + k, m * P:(m + 1) * P], panelv(2)[:, k, :], start=k == 0, stop=False)
                ins.then_inc(free[2], 1)

            def out_quarter(n, q):
                at = 4 * n + q - 2
                w = w_part[at % 2]
                mix = mix_diff if q >= 2 else mix_hgrn
                pe.wait_ge(mix_low, 2 if q >= 2 else 1)
                if q == 0 and n > 1:
                    pe.wait_ge(wout_read, NT * (n - 1))
                pe.wait_ge(w_high, at + 1)
                pe.wait_ge(w_low, at + 1)
                order = [(k, m) for m in range(NT) for k in range(4)] if q == 3 else [(k, m) for k in range(4) for m in range(NT)]
                for k, m in order:
                    kk = 4 * (q % 2) + k
                    for part, (a, b) in enumerate(((0, 0), (0, 1), (1, 0))):
                        ins = mm(pw[2 * (n % 2) + m][:, :], mix[:, a, kk, m * P:(m + 1) * P], w[:, b, k, :],
                                 start=q == 0 and k == 0 and part == 0, stop=q == 3 and k == 3 and part == 2)
                    if q == 3 and k == 3:
                        ins.then_inc(wout_done, 1)
                if q < 3:
                    ins.then_inc(w_used, 1)

            used = ADA0 + 7 * NG
            for n in range(NP_D):
                if n == 0:
                    out_first_half()
                for q in range(2 if n == 0 else 0, 4):
                    out_quarter(n, q)
                if n in (1, 2):
                    pe.wait_ge(ada_a, GIVEN + used + n)
                    ada_spread(n - 1, AUX_O + n - 1)

            pe.wait_ge(xn_ready, 2 * NT)
            pe.wait_ge(aux_read, GIVEN + AUX_O + 2)
            pe.wait_ge(wout_read, 8)
            for q in range(KT // 2):
                for k in range(2):
                    for m in range(NT):
                        ins = pe.transpose(bank[q][:, k * SEQ + m * P:k * SEQ + (m + 1) * P],
                                           xn2[:, m, (2 * q + k) * P:(2 * q + k + 1) * P], ident)
                ins.then_inc(xt_full, 1)
            pe.wait_ge(wr_loaded, 16)
            for k in range(KT):
                q = k // 2
                pe.wait_ge((xt_a, xt_v)[q % 2], 4 + q // 2 + 1)
                ins = mm(bank[0][32 * (k % 4):32 * (k % 4) + 32, 0:SEQ], wr[:, k, :], h2T[:, k, :], start=k < 4, stop=k >= KT - 4)
            ins.then_inc(rt_pe, 1)
            pe.wait_ge(rt_act, 1)
            for m in range(NT):
                ins = pe.transpose(bank[1][:, m * P:(m + 1) * P], lt[:, m * P:(m + 1) * P], ident)
            ins.then_inc(rt_pe, 1)
            pe.wait_ge(chosen_ready, 1)
            mm(bank[2][:, 0:NE], before, chosen[:, 0, :])
            mm(bank[2][:, NE:2 * NE], ones[:, :], chosen[:, 0, :], stop=False)
            mm(bank[2][:, NE:2 * NE], before, chosen[:, 1, :], start=False)
            mm(bank[2][:, 2 * NE:3 * NE], ones[:, :], chosen[:, 0, :], stop=False)
            mm(bank[2][:, 2 * NE:3 * NE], ones[:, :], chosen[:, 1, :], start=False).then_inc(rt_pe, 1)

            def experts(n, r):
                half = [slice(0, CAP), slice(CAP, P)]
                pe.wait_ge(sel_ready, n + r + 1)
                def gather(j):
                    b = j % 2
                    pe.wait_ge(m_read[b], GIVEN + 3 * n + j // 2)
                    for kk in range(4):
                        k = 4 * j + kk
                        for m in range(NT):
                            ins = mm(hx[b][:, kk * P:(kk + 1) * P], xn2[:, m, k * P:(k + 1) * P], sel[:, m, :],
                                     start=m == 0, stop=m == NT - 1)
                    ins.then_inc(m_full[b], 1)

                def gathered_gates():
                    pe.wait_ge(m_read[0], GIVEN + 3 * n + 2)
                    for m in range(NT):
                        ins = pe.transpose(hx[0][:, m * P:(m + 1) * P], selg[:, m, :], ident)
                    ins.then_inc(m_full[0], 1)

                def expert_part(o, q, s, filled, done):
                    pe.wait_ge(efull[s], filled)
                    wp = slotv(s).rearrange("p (e k n) -> p e k n", e=2, k=4)
                    for kk in range(4):
                        k = 4 * q + kk
                        for e in range(2):
                            ins = mm(o[half[e], :], xe[:, k, half[e]], wp[:, e, kk, :], start=k == 0, stop=k == KT - 1)
                    ins.then_inc(done if q == 3 else efree[s], 1)

                gather(0)
                gather(1)
                pe.wait_ge(hid_ready, GIVEN + n)
                for q in range(4):
                    pe.wait_ge(m_read[q % 2], GIVEN + 3 * n + q // 2 + 1)
                    expert_part(acc, q, q, 32 * (2 * n + 1 if q else n + 1), gate_done)
                    if q < 2:
                        gather(q + 2)
                    elif q == 2:
                        gathered_gates()
                for q, (s, filled) in enumerate(((4, 32 * (2 * n + 1)), (5, 32 * (2 * n + 1)), (6, 32 * (n + 1)), (1, 32 * (2 * n + 2)))):
                    expert_part(aux, q, s, filled, up_done)
                pe.wait_ge(hid_ready, GIVEN + n + 1)
                pe.wait_ge(m_read[1], GIVEN + 3 * n + 2)
                for f in range(FT):
                    ins = pe.transpose(hx[1][:, f * P:(f + 1) * P], hid[:, f * P:(f + 1) * P], ident)
                ins.then_inc(m_full[1], 1)
                pe.wait_ge(m_read[1], GIVEN + 3 * n + 3)
                pe.wait_ge(sc_read, GIVEN + 8 * n)
                for f, s in enumerate((2, 3, 4, 5)):
                    pe.wait_ge(efull[s], 32 * (2 * n + 2))
                    wp = ring[:, s, :].rearrange("p (e n) -> p e n", e=2)
                    for dc in range(NP_D):
                        for e in range(2):
                            ins = mm(pw[dc][half[e], :], hidT[:, f, half[e]], wp[:, e, dc * PANEL:(dc + 1) * PANEL],
                                     start=f == 0, stop=f == FT - 1)
                        if f == FT - 1:
                            ins.then_inc(y_done, 1)
                    if f < FT - 1:
                        ins.then_inc(efree[s], 1)
                pe.wait_ge(m_read[0], GIVEN + 3 * n + 3)
                pe.wait_ge(y_gated, NP_D * n + NP_D)
                for m in range(NT):
                    for dc in range(NP_D):
                        if m:
                            pe.wait_ge(sc_read, GIVEN + 8 * n + dc + 1)
                        mm(pw[dc][:, :], selT[:, m * P:(m + 1) * P], ys[:, dc * PANEL:(dc + 1) * PANEL]).then_inc(sc_done, 1)

            with pe.Fori(0, NPAIR) as i:
                experts(i, 0)
            pe.wait_ge(routed, 1)
            most = pe.value_load(count_i[0:1, 0:1], min_val=0, max_val=SEQ)
            with pe.If(most > CAP):
                with pe.Fori(1, ROUNDS) as r:
                    with pe.Fori(0, NPAIR) as i:
                        experts(r * NPAIR + i, r)

        @block.scalar
        def _(act):
            small = lambda dst, src: act.dma_start(dst, src).then_inc(s_small, 16)
            small(cst[:, :], consts)
            small(rows[ROW_C:ROW_AN, :], c.rearrange("o (k p) -> (o k) p", p=P))
            small(rows[ROW_AN:ROW_FN, :], attn_norm.rearrange("o (k p) -> (o k) p", p=P))
            small(rows[ROW_FN:ROW_LB, :], ffn_norm.rearrange("o (k p) -> (o k) p", p=P))
            small(rows[ROW_LB:ROW_SUB, :], hgrn_lb.rearrange("o (k p) -> (o k) p", p=P))
            small(rows[ROW_SUB:ROW_HN, :], diff_subln)
            small(rows[ROW_HN:N_ROWS, :], hgrn_norm)
            bm = b_ada.rearrange("o (k p) -> (o k) p", p=P)
            small(brows[0:2 * KT, :], bm[0:2 * KT, :])
            small(brows[2 * KT:4 * KT, :], bm[3 * KT:5 * KT, :])

            act.wait_ge(s_x, 32)
            for m in range(NT):
                act.activation(xn[:, m, :], res[:, m, :], ACT.Square, accum_out=stat[:, m:m + 1]).then_inc(sumsq, 1)
            act.wait_ge(pre_t, 1)
            act.activation(cols[:, :], aux[:, 0:N_ROWS], ACT.Copy).then_inc(pre_v, 1)
            act.wait_ge(pre_v, 1)
            act.activation(stat[:, 24:24 + KT], cols[:, ROW_C:ROW_C + KT], ACT.Exp, scale=-1.0).then_inc(pre_v, 1)
            act.wait_ge(pre_t, 2)
            act.activation(bcols[:, :], acc[:, 0:64], ACT.Copy).then_inc(pre_v, 1)
            act.wait_ge(pre_t, 3)
            act.activation(work[0:2 * NH, 6656:6656 + BIAS_W], hx[1][0:2 * NH, 0:BIAS_W], ACT.Copy).then_inc(brow_ready, 1)
            act.wait_ge(pre_d, 1)
            act.activation(lams[0:1, 2:4], lams[0:1, 0:2], ACT.Exp).then_inc(pre_v, 1)
            act.wait_ge(pre_d, 2)
            act.activation(lb[:, 1, :], lb[:, 0, :], ACT.Exp).then_inc(pre_v, 1)
            act.wait_ge(pre_t, 4)
            act.activation(stat[:, 4:5], hx[0][:, 0:1], ACT.Copy, scale=-1.0).then_inc(pre_v, 1)
            for q in range(0, KT // 2, 2):
                act.wait_ge(xt_full, q + 1)
                act.activation(hT[:, 2 * q:2 * q + 2, :].rearrange("p k t -> p (k t)"), pw[q % 4][:, :], ACT.Copy).then_inc(xt_a, 1)

            def copy_row(done, value):
                act.wait_ge(done, GIVEN + value)
                act.activation(arow[0], acc[:, :], ACT.Copy).then_inc(ada_copied, 1)

            with act.Fori(0, ADA0) as i:
                copy_row(ada_a, i + 1)
                copy_row(ada_b, i + 1)

            act.wait_ge(mod_ready, 1)
            act.wait_ge(xt_a, KT // 4)
            act.wait_ge(xt_v, KT // 4)
            for k in range(KT // 2, KT):
                ins = act.activation(hT[:, k, :], hT[:, k, :], ACT.Identity, scale=a_mul[:, k:k + 1], bias=mod[:, k:k + 1])
            ins.then_inc(h_ready2, 1)

            backwards = lambda t: t.rearrange("p (c n) -> p c n", n=P)[:, :, ::-1]

            def copy_banks(w0, dst):
                for b in range(GH):
                    act.wait_ge(win_done, GIVEN + w0 + b + 1)
                    act.activation(dst[:, b * SEQ:(b + 1) * SEQ], pw[b][:, 0:SEQ], ACT.Copy).then_inc(win_read, 1)

            def copy_queries(w0, dst):
                for b in range(GH):
                    act.wait_ge(win_done, GIVEN + w0 + b + 1)
                    act.activation(dst[:, b * SEQ:(b + 1) * SEQ].rearrange("p (c n) -> p c n", n=P),
                                   backwards(pw[b][:, 0:SEQ]), ACT.Copy, scale=float(QK) ** -0.5).then_inc(win_read, 1)

            def copy_values(w0, dst):
                for m in range(NT):
                    act.wait_ge(win_done, GIVEN + w0 + m + 1)
                    act.activation(toks(dst)[:, m, :], pw[m][:, :], ACT.Copy).then_inc(win_read, 1)

            def head_outputs(used, dst, square):
                for h in range(GH):
                    b = h % 2
                    act.wait_ge(hx_full[b], used[b] + h // 2 + 1)
                    at = slice(h * SEQ, (h + 1) * SEQ)
                    act.activation(dst[:, at], hx[b][:, 0:SEQ], ACT.Copy)
                    act.activation(square[:, at], hx[b][:, 0:SEQ], ACT.Square).then_inc(hx_read[b], 1)

            def rstd(read, n, src, dst):
                act.wait_ge(aux_read, GIVEN + read)
                act.activation(dst, src, ACT.Ln).then_inc(or_log, 1)
                act.wait_ge(or_log, n + 1)
                act.activation(dst, dst, ACT.Exp, scale=-0.5).then_inc(or_ready, 1)

            with act.Fori(0, NG) as i:
                w0 = WIN_G * i
                act.wait_ge(hgrn_out, GIVEN + i)
                copy_banks(w0, dbuf[0])
                act.wait_ge(f_clamped, i + 1)
                act.activation(zbuf[0], dbuf[1], ACT.Exp, scale=-1.0).then_inc(f_exp, 1)
                act.wait_ge(f_split, i + 1)
                act.activation(zbuf[0], dbuf[1], ACT.Ln).then_inc(f_log, 1)
                act.activation(zbuf[1], dbuf[0], ACT.Ln, scale=1.0 / SPLIT).then_inc(f_log, 1)
                copy_banks(w0 + GH, qh)
                for lv, n in enumerate(LEVELS[1:] + [P]):
                    act.wait_ge(d_ready, 8 * i + lv + 1)
                    d = dbuf[lv % 2]
                    if n < CHUNK:
                        act.activation(d, d, ACT.Exp).then_inc(e_ready, 1)
                    elif n == CHUNK:
                        d4, b4 = (t.rearrange("p (q s n) -> p q s n", s=2, n=n) for t in (d, bh))
                        act.activation(d4[:, :, 0, :], d4[:, :, 0, :], ACT.Exp)
                        act.activation(d4[:, :, 1, :], b4[:, :, 1, :], ACT.Exp).then_inc(e_ready, 1)
                    else:
                        d4, b4 = (t.rearrange("p (h c n) -> p h c n", c=4, n=CHUNK) for t in (d, bh))
                        act.activation(d4[:, :, 0:2, :], d4[:, :, 0:2, :], ACT.Exp)
                        act.activation(d4[:, :, 3, :], d4[:, :, 3, :], ACT.Exp)
                        act.activation(d4[:, :, 2, :], b4[:, :, 2, :], ACT.Exp).then_inc(e_ready, 1)
                    if lv == 4:
                        copy_values(w0 + 2 * GH, vh)
                head_outputs([HX_G[b] * i + 9 - b for b in range(2)], ohb, zbuf[0])
                copy_banks(w0 + 2 * GH + NT, gh)
                act.wait_ge(g_clamped, i + 1)
                act.activation(zbuf[1], zbuf[1], ACT.Exp, scale=-1.0).then_inc(g_exp, 1)
                rstd(AUX_G + 6 * i + 5, i, dbuf[0], dbuf[1])

            def split_high(high, source, done):
                act.activation(high, source, ACT.Copy).then_inc(done, 1)

            act.wait_ge(hgrn_out, GIVEN + NG)
            split_high(mix_hgrn[:, 0, :, :], mixT[:, KT // 2:KT, :], mix_high)
            with act.Fori(0, NG) as j:
                w0 = WIN_G * NG + WIN_A * j
                a0 = AUX_A + 9 * j
                act.wait_ge(diff_out, GIVEN + j)
                copy_queries(w0, qd)
                copy_banks(w0 + GH, kd)
                def probs_forward(h):
                    act.wait_ge(aux_full, a0 + 4 + h)
                    act.activation(aT[:, h, :].rearrange("p (c n) -> p c n", n=P), backwards(aux[:, 0:3 * P]),
                                   ACT.Copy).then_inc(aux_read, 1)

                for h in range(GH):
                    act.wait_ge(max_ready, GH * j + h + 1)
                    for s in range(2):
                        for q, (at, n) in enumerate(((0, SEQ), (SEQ, P))):
                            v = sbuf[:, h % 2, s, at:at + n]
                            ins = act.activation(v, v, ACT.Exp, bias=hstat[:, h % 2, 2 * q + s:2 * q + s + 1],
                                                 accum_out=hstat[:, h % 2, 4 + 2 * q + s:5 + 2 * q + s])
                    ins.then_inc(p_ready, 1)
                    if h:
                        probs_forward(h - 1)
                probs_forward(GH - 1)
                copy_values(w0 + 2 * GH, vd)
                act.wait_ge(a_ready, GH * j + GH)
                head_outputs([hx_base[b] + HX_A * j + 4 for b in range(2)], odb, osq_d)
                rstd(a0 + 9, NG + j, rs_d, rs_d)

            act.wait_ge(diff_out, GIVEN + NG)
            act.wait_ge(wr_zeroed, 1)
            act.dma_start(wr[:, :, 0:NE], w_router.rearrange("(k p) e -> p k e", p=P)).then_inc(wr_loaded, 16)
            def square_chunk(q):
                n, m = q // NT, q % NT
                act.wait_ge(res_ready, q + 1)
                if q >= len(squares):
                    act.wait_ge(sumsq, NT + q + 1 - len(squares))
                act.activation(squares[q % len(squares)], res[:, m, n * PANEL:(n + 1) * PANEL], ACT.Square,
                               accum_out=stat[:, 52 + m * NP_D + n:53 + m * NP_D + n]).then_inc(sumsq, 1)

            split_high(mix_diff[:, 0, :, :], mixT[:, 0:KT // 2, :], mix_high)
            for at in range(4 * NP_D - 2):
                n, q = (at + 2) // 4, (at + 2) % 4
                act.wait_ge(full[w_slot(n, q)], w_filled(n, q))
                if at >= 2:
                    act.wait_ge(wout_done if at % 4 == 3 else w_used, w_released(at - 2))
                split_high(w_part[at % 2][:, 0, :, :], panelv(w_slot(n, q))[:, 4 * (q % 2):4 * (q % 2) + 4, :], w_high)
                if n and q == 3:
                    for m in range(NT):
                        square_chunk(NT * (n - 1) + m)
            for m in range(NT):
                square_chunk(NT * (NP_D - 1) + m)
            act.wait_ge(rstd_ready, 2)
            act.activation(xn2[:, 1, :], res[:, 1, :], ACT.Copy, scale=stat[:, 3:4]).then_inc(xn_ready, 1)
            for q in range(0, KT // 2, 2):
                act.wait_ge(xt_full, KT // 2 + q + 1)
                for k in (2 * q, 2 * q + 1):
                    ins = act.activation(h2T[:, k, :], bank[q][:, (k % 2) * SEQ:(k % 2 + 1) * SEQ], ACT.Identity,
                                         scale=a_mul[:, KT + k:KT + k + 1], bias=mod[:, 2 * KT + k:2 * KT + k + 1])
                ins.then_inc(xt_a, 1)
            act.wait_ge(wout_read, NT * NP_D)
            act.dma_start(fnorm, final_norm.rearrange("(o d) -> o d", o=1).to_broadcast([P, D])).then_inc(fn_loaded, 16)
            act.wait_ge(rt_pe, 1)
            act.activation(lt, bank[0][:, 0:SEQ], ACT.Copy).then_inc(rt_act, 1)
            act.wait_ge(rt_dve, 1)
            act.activation(prob, prob, ACT.Exp).then_inc(rt_act, 1)

            def experts(n):
                for j in (0, 2):
                    act.wait_ge(m_full[0], 3 * n + j // 2 + 1)
                    for kk in range(4):
                        k = 4 * j + kk
                        ins = act.activation(xe[:, k, :], hx[0][:, kk * P:(kk + 1) * P], ACT.Identity,
                                             scale=a_mul[:, KT + k:KT + k + 1], bias=mod[:, 2 * KT + k:2 * KT + k + 1])
                    ins.then_inc(m_read[0], 1)
                act.wait_ge(m_full[0], 3 * n + 3)
                act.activation(selT, hx[0][:, 0:SEQ], ACT.Copy).then_inc(m_read[0], 1)
                act.wait_ge(gate_clamped, n + 1)
                act.activation(hid, hid, ACT.Exp, scale=-1.0).then_inc(gate_exp, 1)
                act.wait_ge(m_full[1], 3 * n + 3)
                act.activation(hidT[:, :, :], hx[1][:, :].rearrange("p (f s) -> p f s", f=FT), ACT.Copy).then_inc(m_read[1], 1)

            with act.Fori(0, NPAIR) as i:
                experts(i)
            act.wait_ge(routed, 1)
            most = act.value_load(count_i[0:1, 0:1], min_val=0, max_val=SEQ)
            with act.If(most > CAP):
                with act.Fori(1, ROUNDS) as r:
                    with act.Fori(0, NPAIR) as i:
                        experts(r * NPAIR + i)
            act.wait_ge(moe_out, 1)
            for m in range(NT):
                act.activation(xn2[:, m, :], res[:, m, :], ACT.Square, accum_out=stat[:, m:m + 1]).then_inc(sumsq, 1)

        @block.vector
        def _(dve):
            ch = Chain(dve, c_dve)
            tt, ts, stt = dve.tensor_tensor, dve.tensor_scalar, dve.scalar_tensor_tensor
            dve.memset(ones[:, :], 1.0)
            dve.memset(mean_w[:, :], 1.0 / HD)
            dve.memset(cact[:, :, :], 0.0)
            dve.memset(sc_diag, 0.0)
            dve.memset(pos[:, :, :], -1.0)
            dve.memset(gate[:, :, :], 0.0)
            dve.memset(relb[BUCKETS:BUCKETS + 1, :], 1.0)
            ch.link(dve.memset(resets[:, :], 1.0))
            dve.memset(resets[:, 0:SEQ:CHUNK], 0.0).then_inc(s_const, 1)
            dve.wait_ge(s_const, 1)
            dve.wait_ge(sumsq, NT)
            ts(stat[:, 2:4], stat[:, 0:2], 1.0 / D, EPS, ALU.mult, ALU.add).then_inc(var_ready, 1)
            dve.wait_ge(s_small, 16 * 17)
            dve.tensor_copy(msk[:, :, :].rearrange("p l n -> p (l n)"), work[:, 0:len(LEVELS) * P]).then_inc(mask_ready, 1)
            ch.link(tt(lam[0:1, 0:2, :], lam[0:1, 0:2, :], lam[0:1, 2:4, :], ALU.mult))
            dve.reduce_sum(lams[0:1, 0:2], lam[0:1, 0:2, :], axis=AX).then_inc(pre_d, 1)
            dve.wait_ge(rstd_ready, 1)
            for m in range(NT):
                ts(xn[:, m, :], res[:, m, :], stat[:, 2 + m:3 + m], None, ALU.mult).then_inc(xn_ready, 1)
            dve.wait_ge(pre_v, 1)
            lbc = cols[:, ROW_LB:ROW_LB + NH]
            tt(lb[:, 0, :], lbc, lbc, ALU.subtract).then_inc(pre_d, 1)
            dve.wait_ge(pre_v, 2)
            ch.link(ts(stat[:, 24:24 + KT], stat[:, 24:24 + KT], 1.0, None, ALU.add))
            ch.link(dve.reciprocal(stat[:, 24:24 + KT], stat[:, 24:24 + KT]))
            ch.link(tt(ccol[:, :], stat[:, 24:24 + KT], cols[:, ROW_C:ROW_C + KT], ALU.mult))
            dve.tensor_copy(cact[:, :, 0], ccol[:, :]).then_inc(cact_ready, 1)
            dve.wait_ge(pre_v, 4)
            stt(lams[0:1, 4:5], lams[0:1, 2:3], LAMBDA_INIT, lams[0:1, 3:4], ALU.add, ALU.subtract).then_inc(lam_ready, 1)
            dve.wait_ge(pre_v, 5)
            ch.link(dve.reciprocal(lb[:, 2, :], lb[:, 1, :]))
            ch.link(tt(lb[:, 3, :], lb[:, 1, :], lb[:, 2, :], ALU.mult))
            ch.link(tt(lb[:, 4, :], lb[:, 3, :], lb[:, 3, :], ALU.subtract))
            ch.link(ts(lb[:, 4, :], lb[:, 4, :], 0.0, None, ALU.max))
            ch.step(ts(lb[:, 0, :], lb[:, 4, :], -1.0, 1.0, ALU.mult, ALU.add))
            ch.link(ts(cols[:, ROW_SUB:ROW_SUB + 1], cols[:, ROW_SUB:ROW_SUB + 1], 1.0 - LAMBDA_INIT, None, ALU.mult))
            for q in range(1, KT // 2, 2):
                dve.wait_ge(xt_full, q + 1)
                dve.tensor_copy(hT[:, 2 * q:2 * q + 2, :].rearrange("p k t -> p (k t)"), pw[q % 4][:, :]).then_inc(xt_v, 1)

            def sum_columns(use, col):
                dve.wait_ge(aux_full, use + 1)
                part = aux[:, :].rearrange("p (q n) -> p q n", q=4)
                dve.reduce_sum(mod[:, bass.ds(col, 4)], part, axis=AX).then_inc(aux_read, 1)

            def sum_panel(n, row, posted, parts=range(4)):
                for part in parts:
                    half = part // 2
                    if part == 0:
                        dve.wait_ge(aux_full, posted)
                    if part % 2 == 0:
                        dve.wait_ge(ada_full[half], 16 * (n - ADA0 + 1))
                    for k in range(part % 2 * 4, part % 2 * 4 + 4):
                        kk = 8 * half + k
                        if kk == 0:
                            ins = ts(arow[row], panelv(half)[:, k, :], ccol[:, kk:kk + 1], None, ALU.mult)
                        else:
                            ins = stt(arow[row], panelv(half)[:, k, :], ccol[:, kk:kk + 1], arow[row], ALU.mult, ALU.add)
                        if k < 7:
                            ch.link(ins)
                        elif half == 0:
                            ins.then_inc(free[0], 1)
                            dve.wait_ge(free[0], GIVEN + n + 1)
                        else:
                            ins.then_inc(ada_a, 1)

            with dve.Fori(0, ADA0) as i:
                for t in range(2):
                    sum_columns(2 * i + t, 8 * i + 4 * t)
            dve.wait_ge(aux_read, GIVEN + AUX_G)
            dve.wait_ge(pre_v, 3)
            ch.link(tt(mod[:, 0:2 * KT], mod[:, 0:2 * KT], bcols[:, 0:2 * KT], ALU.add))
            stt(a_mul[:, 0:KT], mod[:, KT:2 * KT], 1.0, cols[:, ROW_AN:ROW_AN + KT], ALU.add, ALU.mult).then_inc(mod_ready, 1)
            dve.wait_ge(mod_ready, 1)
            dve.wait_ge(xt_a, KT // 4)
            dve.wait_ge(xt_v, KT // 4)
            for k in range(KT // 2):
                ins = ts(hT[:, k, :], hT[:, k, :], a_mul[:, k:k + 1], mod[:, k:k + 1], ALU.mult, ALU.add)
                if k % 4 == 3:
                    ins.then_inc(h_ready, 1)

            dve.wait_ge(brow_saved, 16)
            with dve.Fori(0, NG) as i:
                ch.enter(i, PER_HGRN)
                w0 = WIN_G * i
                u0 = AUX_G + 6 * i
                n0 = ADA0 + 4 * i
                sum_panel(n0, 0, u0 - 3)
                dve.wait_ge(win_read, GIVEN + w0 + GH)
                ts(dbuf[1], dbuf[0], -CLAMP, CLAMP, ALU.max, ALU.min).then_inc(f_clamped, 1)
                sum_columns(u0, 2 * KT + 16 * i)
                dve.wait_ge(f_exp, i + 1)
                ch.link(ts(zbuf[1], zbuf[0], 1.0, None, ALU.add))
                ch.link(dve.reciprocal(zbuf[1], zbuf[1]))
                for h in range(GH):
                    hd = i * GH + h
                    at = slice(h * SEQ, (h + 1) * SEQ)
                    stt(kh[:, at], zbuf[0][:, at], lb[:, 0, bass.ds(hd, 1)], zbuf[1][:, at], ALU.mult, ALU.mult)
                    ch.step(ts(dbuf[0][:, at], zbuf[1][:, at], lb[:, 0, bass.ds(hd, 1)], lb[:, 4, bass.ds(hd, 1)], ALU.mult, ALU.add))
                ch.wait()
                ts(dbuf[1], dbuf[0], SPLIT, None, ALU.max)
                ts(dbuf[0], dbuf[0], TINY, SPLIT, ALU.max, ALU.min).then_inc(f_split, 1)
                dve.wait_ge(f_log, 2 * i + 2)
                ch.link(tt(dbuf[0], zbuf[0], zbuf[1], ALU.add))
                for h in range(GH):
                    at = slice(h * SEQ, (h + 1) * SEQ)
                    ins = dve.tensor_tensor_scan(bh[:, at], resets[:, :], dbuf[0][:, at], 0.0, ALU.mult, ALU.add)
                ins.then_inc(b_ready, 1)
                sum_panel(n0 + 1, 1, u0)

                def decay(lv, n):
                    dve.wait_ge(e_ready, 8 * i + lv + 1)
                    z4, d4, k4, q4 = (t.rearrange("p (q s n) -> p q s n", s=2, n=n) for t in (zbuf[lv % 2], dbuf[lv % 2], kh, qh))
                    tt(z4[:, :, 0, :], k4[:, :, 0, :], d4[:, :, 0, :], ALU.mult)
                    tt(z4[:, :, 1, :], q4[:, :, 1, :], d4[:, :, 1, :], ALU.mult).then_inc(z_ready, 1)

                def keep(level):
                    for b in range(2):
                        dve.wait_ge(hx_full[b], HX_G[b] * i + level + 1)
                        dst = sc_diag[:, b * 4 * P:(b + 1) * 4 * P].rearrange("p (q n) -> p q n", n=P)
                        ch.step(dve.memset(waiter[:, 2 * level + b:2 * level + b + 1], 0.0))
                        own = msk[:, level:level + 1, :].to_broadcast([P, 4, P])
                        dve.copy_predicated(dst, own, hx[b][:, :].rearrange("p (q n) -> p q n", n=P)).then_inc(hx_read[b], 1)

                halves = LEVELS[1:] + [P]
                dve.wait_ge(mask_ready, 1)
                dve.wait_ge(win_read, GIVEN + w0 + 2 * GH)
                decay(0, halves[0])
                decay(1, halves[1])
                sum_columns(u0 + 1, 2 * KT + 16 * i + 4)
                keep(0)
                for level in range(1, 8):
                    keep(level)
                    if level + 1 < 8:
                        decay(level + 1, halves[level + 1])
                    if level < 5:
                        sum_panel(n0 + 2, 0, u0 + 1, [level - 1])
                dve.wait_ge(hx_full[0], HX_G[0] * i + 9)
                dve.tensor_copy(sc_off, hx[0][:, :]).then_inc(hx_read[0], 1)
                sum_columns(u0 + 2, 2 * KT + 16 * i + 8)
                sum_panel(n0 + 3, 1, u0 + 2)
                for q in range(2):
                    dve.wait_ge(aux_full, u0 + 4 + q)
                    ts(dbuf[0][:, q * PANEL:(q + 1) * PANEL], aux[:, :], EPS, None, ALU.add).then_inc(aux_read, 1)
                dve.wait_ge(win_read, GIVEN + w0 + WIN_G)
                ts(zbuf[1], gh, -CLAMP, None, ALU.max).then_inc(g_clamped, 1)
                sum_columns(u0 + 5, 2 * KT + 16 * i + 12)
                dve.wait_ge(g_exp, i + 1)
                ch.link(ts(zbuf[1], zbuf[1], 1.0, None, ALU.add))
                ch.link(dve.reciprocal(zbuf[1], zbuf[1]))
                ch.link(stt(gh, gh, cols[:, ROW_HN:ROW_HN + 1], zbuf[1], ALU.mult, ALU.mult))
                dve.wait_ge(or_ready, i + 1)
                for b in range(2):
                    dve.wait_ge(hx_read[b], GIVEN + HX_G[b] * (i + 1))
                ch.link(tt(ohb, ohb, dbuf[1], ALU.mult))
                tt(mixT[:, bass.ds(NH + GH * i, GH), :].rearrange("p h t -> p (h t)"), ohb, gh, ALU.mult).then_inc(hgrn_out, 1)
                ch.leave(NG)

            dve.wait_ge(s_bload, 32)

            def add_gate(use, col):
                dve.wait_ge(aux_full, use + 1)
                g = gates_bc[:, bass.ds(col, PANEL)]
                tt(g, aux[:, :], g, ALU.add).then_inc(aux_read, 1)

            def split_low(low, source, high, done):
                tt(low, source, high.bitcast(F32), ALU.subtract).then_inc(done, 1)

            dve.wait_ge(mix_high, 1)
            split_low(mix_hgrn[:, 1, :, :], mixT[:, KT // 2:KT, :], mix_hgrn[:, 0, :, :], mix_low)
            with dve.Fori(0, NG) as j:
                ch.enter(j, PER_DIFF)
                a0 = AUX_A + 9 * j
                n0 = ADA0 + 4 * NG + 3 * j
                sum_panel(n0, 0, a0)
                sum_panel(n0 + 1, 1, a0)
                add_gate(a0, 3 * j * PANEL)
                sum_panel(n0 + 2, 0, a0 + 1)
                add_gate(a0 + 1, (3 * j + 1) * PANEL)

                def biased(h):
                    b = h % 2
                    if h >= 2:
                        dve.wait_ge(a_ready, GH * j + h - 1)
                    dve.wait_ge(bias_loaded[b], 64 * j + 32 * (h // 2 + 1))
                    for s in range(2):
                        dve.wait_ge(hx_full[s], hx_base[s] + HX_A * j + h + 1)
                        tt(sbuf[:, b, s, :], hx[s][:, 0:3 * P], bias[:, b, s, :], ALU.add).then_inc(hx_read[s], 1)
                    for s in range(2):
                        dve.wait_ge(hx_read[s], GIVEN + hx_base[s] + HX_A * j + h + 1)
                    ch.step(dve.reduce_max(hstat[:, b, 0:2], sbuf[:, b, :, 0:SEQ], axis=AX))
                    ch.link(dve.reduce_max(hstat[:, b, 2:4], sbuf[:, b, :, SEQ:3 * P], axis=AX))
                    ts(hstat[:, b, 0:4], hstat[:, b, 0:4], -1.0, None, ALU.mult).then_inc(max_ready, 1)

                def mixed(h):
                    b = h % 2
                    dve.wait_ge(p_ready, GH * j + h + 1)
                    ch.link(dve.reciprocal(hstat[:, b, 4:8], hstat[:, b, 4:8]))
                    ch.link(ts(hstat[:, b, 5:8:2], hstat[:, b, 5:8:2], stat[:, 4:5], None, ALU.mult))
                    if h:
                        dve.wait_ge(aux_full, a0 + 3 + h)
                    for q, (at, n) in enumerate(((0, SEQ), (SEQ, P))):
                        ch.step(ts(amix[:, at:at + n], sbuf[:, b, 1, at:at + n], hstat[:, b, 5 + 2 * q:6 + 2 * q], None, ALU.mult))
                    ch.wait()
                    for q, (at, n) in enumerate(((0, SEQ), (SEQ, P))):
                        ins = stt(amix[:, at:at + n], sbuf[:, b, 0, at:at + n], hstat[:, b, 4 + 2 * q:5 + 2 * q],
                                  amix[:, at:at + n], ALU.mult, ALU.add)
                    ins.then_inc(a_ready, 1)

                biased(0)
                add_gate(a0 + 2, (3 * j + 2) * PANEL)
                for h in range(1, GH):
                    biased(h)
                    mixed(h - 1)
                mixed(GH - 1)
                for q in range(2):
                    dve.wait_ge(aux_full, a0 + 8 + q)
                    ts(rs_d[:, q * PANEL:(q + 1) * PANEL], aux[:, :], EPS, None, ALU.add).then_inc(aux_read, 1)
                dve.wait_ge(or_ready, NG + j + 1)
                for b in range(2):
                    dve.wait_ge(hx_read[b], GIVEN + hx_base[b] + HX_A * (j + 1))
                stt(mixT[:, bass.ds(GH * j, GH), :].rearrange("p h t -> p (h t)"), odb, cols[:, ROW_SUB:ROW_SUB + 1],
                    rs_d, ALU.mult, ALU.mult).then_inc(diff_out, 1)
                ch.leave(NG)

            dve.wait_ge(diff_out, GIVEN + NG)
            dve.memset(work[:, 5120:5120 + KT * 32], 0.0).then_inc(wr_zeroed, 1)
            ch.link(tt(mod[:, 2 * KT:4 * KT], mod[:, 2 * KT:4 * KT], bcols[:, 2 * KT:4 * KT], ALU.add))
            ch.link(stt(a_mul[:, KT:2 * KT], mod[:, 3 * KT:4 * KT], 1.0, cols[:, ROW_FN:ROW_FN + KT], ALU.add, ALU.mult))
            def out_chunk(q):
                n, m = q // NT, q % NT
                at = slice(n * PANEL, (n + 1) * PANEL)
                dve.wait_ge(wout_done, q + 1)
                if q:
                    dve.wait_ge(res_ready, q)
                tt(tmp, pw[2 * (n % 2) + m][:, :], gates_bc[:, at], ALU.mult).then_inc(wout_read, 1)
                dve.wait_ge(wout_read, q + 1)
                tt(res[:, m, at], res[:, m, at], tmp, ALU.add).then_inc(res_ready, 1)

            for at in range(4 * NP_D - 2):
                n, q = (at + 2) // 4, (at + 2) % 4
                if at == 0:
                    dve.wait_ge(mix_high, 2)
                    split_low(mix_diff[:, 1, :, :], mixT[:, 0:KT // 2, :], mix_diff[:, 0, :, :], mix_low)
                dve.wait_ge(w_high, at + 1)
                if at >= 2:
                    dve.wait_ge(wout_done if at % 4 == 3 else w_used, w_released(at - 2))
                split_low(w_part[at % 2][:, 1, :, :], panelv(w_slot(n, q))[:, 4 * (q % 2):4 * (q % 2) + 4, :],
                          w_part[at % 2][:, 0, :, :], w_low)
                if n and q == 1:
                    for m in range(NT):
                        out_chunk(NT * (n - 1) + m)
                if at in (2, 4, 8, 9):
                    sum_panel(ADA0 + 7 * NG + 1, 1, AUX_O, [(2, 4, 8, 9).index(at)])
                if n >= 2 and q == 2:
                    add_gate(AUX_O + n - 2, (4 + n) * PANEL)
            for m in range(NT):
                out_chunk(NT * (NP_D - 1) + m)
            dve.wait_ge(sumsq, NT + NT * NP_D)
            ch.link(dve.reduce_sum(stat[:, 0:2], stat[:, 52:60].rearrange("p (m n) -> p m n", m=NT), axis=AX))
            ts(stat[:, 2:4], stat[:, 0:2], 1.0 / D, EPS, ALU.mult, ALU.add).then_inc(var_ready, 1)
            dve.wait_ge(rstd_ready, 2)
            dve.wait_ge(res_ready, NT * NP_D)
            ts(xn2[:, 0, :], res[:, 0, :], stat[:, 2:3], None, ALU.mult).then_inc(xn_ready, 1)
            for q in range(1, KT // 2, 2):
                dve.wait_ge(xt_full, KT // 2 + q + 1)
                for k in (2 * q, 2 * q + 1):
                    ins = ts(h2T[:, k, :], bank[q][:, (k % 2) * SEQ:(k % 2 + 1) * SEQ], a_mul[:, KT + k:KT + k + 1],
                             mod[:, 2 * KT + k:2 * KT + k + 1], ALU.mult, ALU.add)
                ins.then_inc(xt_v, 1)

            spread = lambda v, w: v.rearrange("p (m o) -> p m o", o=1).to_broadcast([P, v.shape[1], w])
            m2 = rview(352, 2)
            v1, v2, rs = rview(354, 2), rview(356, 2), rview(358, 2)
            gm = rview(360, 2)
            dve.wait_ge(rt_pe, 2)
            br = stat[:, 8:8 + NE].rearrange("p (o e) -> p o e", o=1).to_broadcast([P, NT, NE])
            parts = bank[1][:, 0:NT * P].rearrange("p (m q n) -> p m n q", m=NT, q=4)[:, :, 0:NE, :]
            ch.link(dve.reduce_sum(logit, parts, axis=AX))
            ch.link(tt(logit, logit, br, ALU.add))
            ch.link(dve.reduce_max(m2, logit, axis=AX))
            tt(prob, logit, spread(m2, NE), ALU.subtract).then_inc(rt_dve, 1)
            dve.wait_ge(rt_act, 2)
            ch.link(dve.reduce_sum(rs, prob, axis=AX))
            ch.link(dve.reciprocal(rs, rs))
            ch.link(tt(prob, prob, spread(rs, NE), ALU.mult))
            g4 = rview(64, 32).rearrange("p (g q) -> p g q", q=EPG)
            ch.step(tt(pair1[:, :, 0:2], g4[:, :, 0:2], g4[:, :, 2:4], ALU.add))
            ch.step(tt(pair1[:, :, 2:4], g4[:, :, 0:4:2], g4[:, :, 1:4:2], ALU.add))
            ch.step(tt(pair1[:, :, 4:5], g4[:, :, 0:1], g4[:, :, 3:4], ALU.add))
            ch.link(tt(pair1[:, :, 5:6], g4[:, :, 1:2], g4[:, :, 2:3], ALU.add))
            ch.link(dve.reduce_max(gsc, pair1, axis=AX))
            grp = lambda t: t.rearrange("p (m g) -> p m g", m=NT)
            ch.link(dve.reduce_max(gm, grp(gsc), axis=AX))
            ch.link(tt(grp(gtmp), grp(gsc), spread(gm, NGRP), ALU.is_equal))
            ch.link(tt(grp(gtmp), grp(gtmp), rank4.rearrange("p (o g) -> p o g", o=1).to_broadcast([P, NT, NGRP]), ALU.mult))
            ch.link(dve.reduce_max(gm, grp(gtmp), axis=AX))
            ch.link(tt(grp(msk4), grp(gtmp), spread(gm, NGRP), ALU.is_equal))
            mk = rview(192, 32).rearrange("p (g q) -> p g q", q=EPG)
            ch.link(tt(mk, g4, spread(msk4, EPG), ALU.mult))
            ch.link(ts(msk4, msk4, -1.0, None, ALU.add))
            ch.link(tt(mk, mk, spread(msk4, EPG), ALU.add))
            r16 = rank16.rearrange("p (o e) -> p o e", o=1).to_broadcast([P, NT, NE])
            for best, value in ((top1, v1), (top2, v2)):
                ch.link(dve.reduce_max(value, masked, axis=AX))
                ch.link(tt(t16, masked, spread(value, NE), ALU.is_equal))
                ch.link(tt(t16, t16, r16, ALU.mult))
                ch.link(dve.reduce_max(gm, t16, axis=AX))
                ch.link(tt(best, t16, spread(gm, NE), ALU.is_equal))
                ch.link(stt(masked, best, -3.0, masked, ALU.mult, ALU.add))
            tt(chosen, top1, top2, ALU.add).then_inc(chosen_ready, 1)
            ch.link(tt(rs, v1, v2, ALU.add))
            ch.link(dve.reciprocal(rs, rs))
            ch.step(tt(v1, v1, rs, ALU.mult))
            ch.link(tt(v2, v2, rs, ALU.mult))
            ch.step(tt(top1, top1, spread(v1, NE), ALU.mult))
            ch.link(tt(top2, top2, spread(v2, NE), ALU.mult))
            ch.link(tt(gate[:, :, 0:NE], top1, top2, ALU.add))
            dve.wait_ge(chosen_ready, 1)
            ch.link(ts(t16, chosen, -1.0, None, ALU.add))
            dve.wait_ge(rt_pe, 3)
            ch.step(dve.reduce_max(stat[:, 5:6], bank[2][:, 2 * NE:3 * NE], axis=AX))
            ch.link(tt(masked, bank[2][:, 0:2 * NE].rearrange("p (m e) -> p m e", m=NT), chosen, ALU.mult))
            ch.link(tt(pos[:, :, 0:NE], masked, t16, ALU.add))
            dve.tensor_copy(count_i[0:1, 0:1], stat[0:1, 5:6]).then_inc(routed, 1)

            def select(e):
                for m in range(NT):
                    for a in range(2):
                        at = slice(a * CAP, (a + 1) * CAP)
                        p1, g1 = pos[:, m, bass.ds(e + a, 1)], gate[:, m, bass.ds(e + a, 1)]
                        ts(sel[:, m, at], slot_id[:, 0:CAP], p1, None, ALU.is_equal)
                        ins = ts(selg[:, m, at], slot_id[:, 0:CAP], p1, g1, ALU.is_equal, ALU.mult)
                ins.then_inc(sel_ready, 1)

            def experts(n, e, ch):
                for j in (1, 3):
                    dve.wait_ge(m_full[1], 3 * n + j // 2 + 1)
                    for kk in range(4):
                        k = 4 * j + kk
                        ins = ts(xe[:, k, :], hx[1][:, kk * P:(kk + 1) * P], a_mul[:, KT + k:KT + k + 1],
                                 mod[:, 2 * KT + k:2 * KT + k + 1], ALU.mult, ALU.add)
                    ins.then_inc(m_read[1], 1)
                dve.wait_ge(gate_done, n + 1)
                ts(hid, acc[:, :], -CLAMP, None, ALU.max).then_inc(gate_clamped, 1)
                dve.wait_ge(gate_exp, n + 1)
                ch.link(ts(hid, hid, 1.0, None, ALU.add))
                ch.link(dve.reciprocal(hid, hid))
                ch.link(tt(hid, acc[:, :], hid, ALU.mult))
                dve.wait_ge(up_done, n + 1)
                tt(hid, aux[:, :], hid, ALU.mult).then_inc(hid_ready, 1)
                dve.wait_ge(m_full[0], 3 * n + 3)
                select(e + 2)
                for dc in range(NP_D):
                    dve.wait_ge(y_done, NP_D * n + dc + 1)
                    tt(ys[:, dc * PANEL:(dc + 1) * PANEL], pw[dc][:, :], gates_bc[:, D + dc * PANEL:D + (dc + 1) * PANEL],
                       ALU.mult).then_inc(y_gated, 1)
                dve.wait_ge(sc_read, GIVEN + 8 * n)
                for q in range(NT * NP_D):
                    m, dc = q // NP_D, q % NP_D
                    at = slice(dc * PANEL, (dc + 1) * PANEL)
                    dve.wait_ge(sc_done, 8 * n + q + 1)
                    tt(res[:, m, at], pw[dc][:, :], res[:, m, at], ALU.add).then_inc(sc_read, 1)

            ch.wait()
            select(0)
            with dve.Fori(0, NPAIR) as i:
                ch.enter(i, PER_EXPERTS)
                experts(i, 2 * i, ch)
                ch.leave(NPAIR)
            dve.wait_ge(routed, 1)
            most = dve.value_load(count_i[0:1, 0:1], min_val=0, max_val=SEQ)
            ch.wait()
            dve.wait_ge(sc_read, GIVEN + 8 * NPAIR)
            with dve.If(most > CAP):
                with dve.Fori(1, ROUNDS) as r:
                    rounds = Chain(dve, c_rounds)
                    rounds.turns = (r - 1) * (1 + NPAIR * PER_EXPERTS)
                    rounds.link(ts(pos[:, :, :], pos[:, :, :], -float(CAP), None, ALU.add))
                    select(0)
                    with dve.Fori(0, NPAIR) as i:
                        rounds.enter(i, PER_EXPERTS)
                        experts(r * NPAIR + i, 2 * i, rounds)
                        rounds.leave(NPAIR)
                    rounds.wait()
                    dve.wait_ge(sc_read, r * (8 * NPAIR) + (GIVEN + 8 * NPAIR))
            dve.nop().then_inc(moe_out, 1)
            dve.wait_ge(sumsq, 2 * NT + NT * NP_D)
            ts(stat[:, 2:4], stat[:, 0:2], 1.0 / D, EPS, ALU.mult, ALU.add).then_inc(var_ready, 1)
            dve.wait_ge(rstd_ready, 3)
            dve.wait_ge(fn_loaded, 16)
            for m in range(NT):
                for at in (slice(0, D // 2), slice(D // 2, D)):
                    stt(res[:, m, at], res[:, m, at], stat[:, 2 + m:3 + m], fnorm[:, at], ALU.mult, ALU.mult).then_inc(out_ready, 1)


_INS = ["x", "c", "w_in", "w_out", "attn_norm", "ffn_norm", "w_ada", "b_ada", "lambda_q1", "lambda_k1", "lambda_q2",
        "lambda_k2", "diff_subln", "hgrn_lb", "hgrn_norm", "rel_bias", "w_router", "b_router", "w_gate", "w_up",
        "w_down", "final_norm"]


def kernel(**inputs):
    import numpy as _np
    import concourse.bacc as _bacc
    from concourse import mybir as _mybir
    from concourse.bass_utils import run_bass_kernel_spmd as _run

    nc = _bacc.Bacc("TRN2", target_bir_lowering=False, num_devices=1)
    arrays, args = {}, {}
    consts = dict(zip(("consts", "masks", "onehot"), shape_constants()))
    for name, a in [(n, _np.ascontiguousarray(inputs[n])) for n in _INS] + list(consts.items()):
        arrays[f"in_{name}"] = a
        args[name] = nc.dram_tensor(f"in_{name}", a.shape, _mybir.dt.from_np(a.dtype), kind="ExternalInput").ap()
    for name in ("x", "w_in", "w_out", "w_ada", "w_gate", "w_up", "w_down"):
        args[name] = args[name][0]
    out = nc.dram_tensor("out_y", (1, SEQ, D), F32, kind="ExternalOutput").ap()
    build_program(nc, out=out[0], **args)
    r = _run(nc, [arrays], core_ids=[0])
    return r.results[0]["out_y"]
```
